# Optimizing a Trainium2 kernel written in Bass

```python
import jax, jax.numpy as jnp
from jax import lax
import numpy as np

D_MODEL = 1024
BATCH = 1
SEQ = 512
DEPTH = 2

HEAD_DIM = 64
FOX_HEADS = 6
SB_HEADS = 6
MLA_HEADS = 4
MLA_Q_RANK = 256
MLA_KV_RANK = 128
MLA_NOPE_DIM = 64
MLA_ROPE_DIM = 32
MLA_V_DIM = 64
ROPE_THETA = 10000.0
FOX_WIDTH = FOX_HEADS * HEAD_DIM
SB_WIDTH = SB_HEADS * HEAD_DIM
MLA_WIDTH = MLA_HEADS * MLA_V_DIM
MIX_WIDTH = FOX_WIDTH + MLA_WIDTH + SB_WIDTH
Q_BLOCK = 128
IN_SPLITS = (FOX_WIDTH, FOX_WIDTH, FOX_WIDTH, FOX_HEADS,
             MLA_Q_RANK, MLA_KV_RANK, MLA_ROPE_DIM,
             SB_WIDTH, SB_WIDTH, SB_WIDTH)
IN_COLS = sum(IN_SPLITS)

PEER_HEADS = 8
PEER_N_KEYS = 128
PEER_N_EXPERTS = PEER_N_KEYS * PEER_N_KEYS
PEER_TOPK = 16
PEER_QUERY_DIM = 256
PEER_HALF = PEER_QUERY_DIM // 2
PEER_CHUNK = 128

NORM_EPS = 1e-6

kernel_name = "hybrid_fox_mla_stickbreak_peer"

def rms_norm(x, g):
    xf = x.astype(jnp.float32)
    y = xf * lax.rsqrt(jnp.mean(xf * xf, axis=-1, keepdims=True) + NORM_EPS)
    return (y * g.astype(jnp.float32)).astype(x.dtype)

def _heads(a, n):
    b, s, _ = a.shape
    return a.reshape(b, s, n, -1).transpose(0, 2, 1, 3)

def _q_block(a, i):
    return lax.dynamic_slice_in_dim(a, i * Q_BLOCK, Q_BLOCK, axis=2)

def _sweep(block_fn, seq):
    outs = lax.map(block_fn, jnp.arange(seq // Q_BLOCK))
    nb, b, h, qb, d = outs.shape
    return outs.transpose(1, 0, 3, 2, 4).reshape(b, nb * qb, h * d)

def rope(x, pos):
    half = x.shape[-1] // 2
    inv_freq = 1.0 / (ROPE_THETA ** (jnp.arange(half, dtype=jnp.float32) / half))
    ang = pos[:, None] * inv_freq[None, :]
    cos, sin = jnp.cos(ang), jnp.sin(ang)
    xf = x.astype(jnp.float32)
    x1, x2 = xf[..., :half], xf[..., half:]
    return jnp.concatenate([x1 * cos - x2 * sin, x1 * sin + x2 * cos], axis=-1).astype(x.dtype)

def forgetting_attention(q, k, v, log_f):
    seq = q.shape[2]
    scale = HEAD_DIM ** -0.5
    c = jnp.cumsum(log_f.astype(jnp.float32), axis=-1)
    s_idx = jnp.arange(seq)

    def block(i):
        qb = _q_block(q, i)
        cb = lax.dynamic_slice_in_dim(c, i * Q_BLOCK, Q_BLOCK, axis=2)
        t_idx = i * Q_BLOCK + jnp.arange(Q_BLOCK)
        logits = (jnp.einsum('bhqd,bhkd->bhqk', qb, k, preferred_element_type=jnp.float32) * scale
                  + cb[..., :, None] - c[..., None, :])
        mask = s_idx[None, :] <= t_idx[:, None]
        p = jax.nn.softmax(jnp.where(mask, logits, -jnp.inf), axis=-1)
        return jnp.einsum('bhqk,bhkd->bhqd', p.astype(v.dtype), v)

    return _sweep(block, seq)

def latent_attention(q_nope, q_rope, k_nope, k_rope, v):
    seq = q_nope.shape[2]
    scale = (MLA_NOPE_DIM + MLA_ROPE_DIM) ** -0.5
    s_idx = jnp.arange(seq)

    def block(i):
        qn, qr = _q_block(q_nope, i), _q_block(q_rope, i)
        t_idx = i * Q_BLOCK + jnp.arange(Q_BLOCK)
        logits = (jnp.einsum('bhqd,bhkd->bhqk', qn, k_nope, preferred_element_type=jnp.float32)
                  + jnp.einsum('bhqd,bkd->bhqk', qr, k_rope, preferred_element_type=jnp.float32)) * scale
        mask = s_idx[None, :] <= t_idx[:, None]
        p = jax.nn.softmax(jnp.where(mask, logits, -jnp.inf), axis=-1)
        return jnp.einsum('bhqk,bhkd->bhqd', p.astype(v.dtype), v)

    return _sweep(block, seq)

def stick_breaking_attention(q, k, v):
    seq = q.shape[2]
    scale = HEAD_DIM ** -0.5
    s_idx = jnp.arange(seq)

    def block(i):
        qb = _q_block(q, i)
        t_idx = i * Q_BLOCK + jnp.arange(Q_BLOCK)
        z = jnp.einsum('bhqd,bhkd->bhqk', qb, k, preferred_element_type=jnp.float32) * scale
        mask = s_idx[None, :] < t_idx[:, None]
        log_keep = jnp.where(mask, jax.nn.log_sigmoid(-z), 0.0)
        later = lax.cumsum(log_keep, axis=3, reverse=True) - log_keep
        weight = jnp.where(mask, jnp.exp(jax.nn.log_sigmoid(z) + later), 0.0)
        return jnp.einsum('bhqk,bhkd->bhqd', weight.astype(v.dtype), v)

    return _sweep(block, seq)

def hybrid_mixer(h, w_in, fgate_b, q_norm_g, w_uq, kv_norm_g, w_ukv,
                 out_norm_fox, out_norm_mla, out_norm_sb, w_out):
    b, s, _ = h.shape
    proj = h @ w_in
    parts, off = [], 0
    for n in IN_SPLITS:
        parts.append(proj[..., off:off + n])
        off += n
    fq, fk, fv, f_logit, c_q, c_kv, k_rope_raw, sq, sk, sv = parts
    pos = jnp.arange(s, dtype=jnp.float32)

    log_f = jax.nn.log_sigmoid((f_logit + fgate_b).astype(jnp.float32)).transpose(0, 2, 1)
    y_fox = forgetting_attention(_heads(fq, FOX_HEADS), _heads(fk, FOX_HEADS), _heads(fv, FOX_HEADS), log_f)

    q_up = _heads(rms_norm(c_q, q_norm_g) @ w_uq, MLA_HEADS)
    q_nope, q_rope = q_up[..., :MLA_NOPE_DIM], rope(q_up[..., MLA_NOPE_DIM:], pos)
    kv_up = _heads(rms_norm(c_kv, kv_norm_g) @ w_ukv, MLA_HEADS)
    k_nope, v_mla = kv_up[..., :MLA_NOPE_DIM], kv_up[..., MLA_NOPE_DIM:]
    k_rope = rope(k_rope_raw, pos)
    y_mla = latent_attention(q_nope, q_rope, k_nope, k_rope, v_mla)

    y_sb = stick_breaking_attention(_heads(sq, SB_HEADS), _heads(sk, SB_HEADS), _heads(sv, SB_HEADS))

    y = jnp.concatenate([rms_norm(y_fox.astype(h.dtype), out_norm_fox),
                         rms_norm(y_mla.astype(h.dtype), out_norm_mla),
                         rms_norm(y_sb.astype(h.dtype), out_norm_sb)], axis=-1)
    return y @ w_out

def peer_ffn(h, w_query, keys1, keys2, u, v):
    b, s, d = h.shape
    t = b * s
    xt = h.reshape(t, d)
    q = (xt @ w_query).reshape(t, PEER_HEADS, PEER_QUERY_DIM)
    s1 = jnp.einsum('thd,kd->thk', q[..., :PEER_HALF], keys1, preferred_element_type=jnp.float32)
    s2 = jnp.einsum('thd,kd->thk', q[..., PEER_HALF:], keys2, preferred_element_type=jnp.float32)
    top1, idx1 = lax.top_k(s1, PEER_TOPK)
    top2, idx2 = lax.top_k(s2, PEER_TOPK)
    cand_score = (top1[..., :, None] + top2[..., None, :]).reshape(t, PEER_HEADS, PEER_TOPK * PEER_TOPK)
    cand_id = (idx1[..., :, None] * PEER_N_KEYS + idx2[..., None, :]).reshape(t, PEER_HEADS, PEER_TOPK * PEER_TOPK)
    best, pos = lax.top_k(cand_score, PEER_TOPK)
    expert_id = jnp.take_along_axis(cand_id, pos, axis=-1)
    gates = jax.nn.softmax(best, axis=-1)

    n_chunks = t // PEER_CHUNK
    xc = xt.reshape(n_chunks, PEER_CHUNK, d)
    idc = expert_id.reshape(n_chunks, PEER_CHUNK, PEER_HEADS, PEER_TOPK)
    gc = gates.reshape(n_chunks, PEER_CHUNK, PEER_HEADS, PEER_TOPK)

    def chunk(args):
        xi, ids, g = args
        act = jnp.einsum('cd,chkd->chk', xi, u[ids], preferred_element_type=jnp.float32)
        a = jax.nn.gelu(act, approximate=False) * g
        return jnp.einsum('chk,chkd->cd', a.astype(v.dtype), v[ids])

    return lax.map(chunk, (xc, idc, gc)).reshape(b, s, d)

def setup_inputs(seed: int = 0) -> dict:
    key = jax.random.key(seed)
    ks = jax.random.split(key, 20)
    f32 = jnp.float32

    def nrm(k, shape, scale):
        return jax.random.normal(k, shape, f32) * scale

    def gain(k, shape):
        return 1.0 + 0.02 * jax.random.normal(k, shape, f32)

    return {
        "x": nrm(ks[0], (BATCH, SEQ, D_MODEL), 1.0),
        "attn_norm_g": gain(ks[1], (DEPTH, D_MODEL)),
        "w_in": nrm(ks[2], (DEPTH, D_MODEL, IN_COLS), D_MODEL ** -0.5),
        "fgate_b": 3.0 + 0.1 * jax.random.normal(ks[3], (DEPTH, FOX_HEADS), f32),
        "mla_q_norm_g": gain(ks[4], (DEPTH, MLA_Q_RANK)),
        "w_uq": nrm(ks[5], (DEPTH, MLA_Q_RANK, MLA_HEADS * (MLA_NOPE_DIM + MLA_ROPE_DIM)), MLA_Q_RANK ** -0.5),
        "mla_kv_norm_g": gain(ks[6], (DEPTH, MLA_KV_RANK)),
        "w_ukv": nrm(ks[7], (DEPTH, MLA_KV_RANK, MLA_HEADS * (MLA_NOPE_DIM + MLA_V_DIM)), MLA_KV_RANK ** -0.5),
        "out_norm_fox": gain(ks[8], (DEPTH, FOX_WIDTH)),
        "out_norm_mla": gain(ks[9], (DEPTH, MLA_WIDTH)),
        "out_norm_sb": gain(ks[10], (DEPTH, SB_WIDTH)),
        "w_out": nrm(ks[11], (DEPTH, MIX_WIDTH, D_MODEL), MIX_WIDTH ** -0.5),
        "ffn_norm_g": gain(ks[12], (DEPTH, D_MODEL)),
        "peer_w_query": nrm(ks[13], (DEPTH, D_MODEL, PEER_HEADS * PEER_QUERY_DIM), D_MODEL ** -0.5),
        "peer_keys1": nrm(ks[14], (DEPTH, PEER_N_KEYS, PEER_HALF), PEER_HALF ** -0.5),
        "peer_keys2": nrm(ks[15], (DEPTH, PEER_N_KEYS, PEER_HALF), PEER_HALF ** -0.5),
        "peer_u": nrm(ks[16], (DEPTH, PEER_N_EXPERTS, D_MODEL), D_MODEL ** -0.5),
        "peer_v": nrm(ks[17], (DEPTH, PEER_N_EXPERTS, D_MODEL), PEER_HEADS ** -0.5),
        "final_norm_g": gain(ks[18], (D_MODEL,)),
    }

def reference(x, attn_norm_g, w_in, fgate_b, mla_q_norm_g, w_uq, mla_kv_norm_g, w_ukv,
              out_norm_fox, out_norm_mla, out_norm_sb, w_out, ffn_norm_g, peer_w_query,
              peer_keys1, peer_keys2, peer_u, peer_v, final_norm_g):
    for l in range(DEPTH):
        h = rms_norm(x, attn_norm_g[l])
        x = x + hybrid_mixer(h, w_in[l], fgate_b[l], mla_q_norm_g[l], w_uq[l], mla_kv_norm_g[l],
                             w_ukv[l], out_norm_fox[l], out_norm_mla[l], out_norm_sb[l], w_out[l])
        h = rms_norm(x, ffn_norm_g[l])
        x = x + peer_ffn(h, peer_w_query[l], peer_keys1[l], peer_keys2[l], peer_u[l], peer_v[l])
    return rms_norm(x, final_norm_g)


_drawn_inputs = setup_inputs


def setup_inputs(seed=0):
    import zlib

    import numpy as np

    out = dict(_drawn_inputs(seed))
    spreads = {}
    factors = {'mla_q_norm_g': 3.091,
     'out_norm_mla': 9.199,
     'final_norm_g': 24.437,
     'out_norm_fox': 7.949,
     'out_norm_sb': 7.988,
     'ffn_norm_g': 4.346}
    for name, (base, spread) in spreads.items():
        noise = np.random.default_rng([zlib.crc32(name.encode()), seed]).standard_normal(out[name].shape)
        drawn = base * np.exp(spread * noise) if base else spread * noise
        out[name] = __import__('jax').numpy.asarray(drawn.astype(out[name].dtype))
    for name, factor in factors.items():
        out[name] = (out[name] * factor).astype(out[name].dtype)
    return out
```

```python
from contextlib import ExitStack

import numpy as np

import concourse.bass as bass
from concourse import mybir

F32 = mybir.dt.float32
BF16 = mybir.dt.bfloat16
U32 = mybir.dt.uint32
ALU = mybir.AluOpType
ACT = mybir.ActivationFunctionType
AX = mybir.AxisListType

P = 128
D = 1024
SEQ = 512
DEPTH = 2
TILES = SEQ // P
STEPS = DEPTH * TILES
KC = D // P
HD = 64
FH, MH, SH = 6, 4, 6
HEADS = FH + MH + SH
FW, MW, SW = FH * HD, MH * HD, SH * HD
QR, KR = 256, 128
NOPE, ROPE = 64, 32
MD = NOPE + ROPE
EPS = 1e-6
NEG = -1e30
GONE = -3.0e38

PH = 8
NK = 128
TOPK = 16
EXPERTS = NK * NK
PICKS = PH * TOPK

C_FQ, C_FK, C_FV, C_FL = 0, FW, 2 * FW, 3 * FW
C_CQ = C_FL + FH
C_KR = C_CQ + QR + KR
C_SQ = C_KR + ROPE
C_SK, C_SV = C_SQ + SW, C_SQ + 2 * SW

WMAX = 384
BLOCKS = ([("in", c, WMAX) for c in (C_FQ, C_FK, C_FV, C_CQ, C_SQ, C_SK, C_SV)]
          + [("out", c, min(WMAX, D - c)) for c in range(0, D, WMAX)]
          + [("q", g * D + c, min(WMAX, D - c)) for g in range(2) for c in range(0, D, WMAX)])
NB = len(BLOCKS)
WSLOTS = 2
assert NB % WSLOTS == 0

K_ID, K_MASK, K_LT, K_IOTA, K_ROPE = 0, 128, 128 + 897, 256 + 897, 272 + 897
KW = K_ROPE + TILES * 2 * (ROPE // 2)

R = 8
G = 4
ITS = PICKS // R
GPI = R // G


class Ring:

    def __init__(self, bufs, fills):
        self.bufs = bufs
        self.labels = [x for x, _ in fills]
        self.by = [e for _, e in fills]
        self.per = {e: self.by.count(e) for e in "av"}

    def slot(self, label):
        return self.labels.index(label) % self.bufs

    def full(self, n, label):
        return n * len(self.labels) + self.labels.index(label) + 1

    def before(self, n, label):
        i = self.labels.index(label) - self.bufs
        if i < 0:
            return None
        e = self.by[i]
        return e, n * self.per[e] + self.by[:i].count(e) + 1


PA = Ring(2, [("fq", "a"), ("fk", "a"), ("fv", "a"), ("cc", "v"), ("kf", "v"), ("sq", "a"), ("sk", "a"),
              ("sv", "a"), ("cum", "v"), ("qup", "v"), ("kvup", "a")]
          + [(f"s{i}", "v") for i in range(HEADS)] + [(f"wo{i}", "v") for i in range(3)]
          + [(f"wq{i}", "a") for i in range(6)])
PB = Ring(2, [("hT0", "v"), ("hT1", "v"), ("ncT", "v"), ("cqT", "v"), ("qTm", "a"), ("kTm", "a")]
          + [(f"p{i}", "a") for i in range(HEADS)]
          + [("yT0", "v"), ("yT1", "v"), ("gT0", "a"), ("gT1", "a")])
PY = Ring(1, [("y", "v"), ("ks0", "a"), ("ks1", "a")])

DVE_LINKS = 89
ACT_LINKS = 26


def trunk(nc, x_d, w_in, fgate_b, attn_gT, lat_gT, out_gT, ffn_g, final_g, w_uq, w_ukv, w_out,
          w_q, keys_T, u_d, v_d, consts_d, out_d):
    with ExitStack() as ctx:
        def sb(name, shape, dt=F32):
            return ctx.enter_context(nc.sbuf_tensor(name, shape, dt))

        def sem(name):
            return ctx.enter_context(nc.semaphore(name))

        x_all = sb("x_all", [P, TILES, D])
        u_ring = sb("u_ring", [P, R, D])
        v_ring = sb("v_ring", [P, R, D])
        h = sb("h", [P, D])
        hT = sb("hT", [P, KC, P])
        h_dot = sb("h_dot", [P, D])
        kT_fox = sb("kT_fox", [P, FH // 2, SEQ])
        kT_sb = sb("kT_sb", [P, SH // 2, SEQ])
        kT_mla = sb("kT_mla", [MD, MH, SEQ])
        v_fox = sb("v_fox", [P, TILES, FW])
        v_sb = sb("v_sb", [P, TILES, SW])
        v_mla = sb("v_mla", [P, TILES, MW])
        qT_fox = sb("qT_fox", [P, FH // 2, P])
        qT_sb = sb("qT_sb", [P, SH // 2, P])
        qT_mla = sb("qT_mla", [MD, MH, P])
        ffn_gain = sb("ffn_gain", [P, DEPTH, D])
        gT_attn = sb("gT_attn", [P, DEPTH, KC])
        gT_out = sb("gT_out", [P, DEPTH, KC])
        gT_lat = sb("gT_lat", [P, DEPTH, 3])
        gate_b = sb("gate_b", [P, DEPTH, FH])
        w_uq_sb = sb("w_uq_sb", [P, DEPTH, 2, MH * MD])
        w_ukv_sb = sb("w_ukv_sb", [P, DEPTH, MH * 2 * HD])
        keys_sb = sb("keys_sb", [P, DEPTH, 2, NK])
        consts = sb("consts", [P, KW])
        w_ring = sb("w_ring", [P, WSLOTS, KC, WMAX])
        w_kf = sb("w_kf", [P, KC, ROPE + FH])
        mask = sb("mask", [P, SEQ + 1])
        scr = sb("scr", [P, 6, SEQ])
        c_all = sb("c_all", [P, TILES + 1, FH])
        c_cur = sb("c_cur", [P, FH])
        ncT = sb("ncT", [FH, SEQ])
        fl = sb("fl", [P, 4, FH])
        stat = sb("stat", [P, 32])
        rsum = sb("rsum", [P, HEADS])
        rinv = sb("rinv", [P, HEADS])
        nmax = sb("nmax", [P, HEADS])
        top = sb("top", [P, 8, TOPK])
        top_i = sb("top_i", [P, 8, TOPK], U32)
        top_f = sb("top_f", [P, 8, TOPK])
        best = sb("best", [P, PH, TOPK])
        pos = sb("pos", [P, 4, TOPK], U32)
        pos_h = sb("pos_h", [P, 2, 4 * TOPK], U32)
        pos_f = sb("pos_f", [P, 2, 4 * TOPK])
        key_f = sb("key_f", [P, 2, 4 * TOPK])
        gsum = sb("gsum", [P, 2, PH])
        ids = sb("ids", [P, PICKS], U32)
        gates = sb("gates", [P, PICKS])
        ids_f = sb("ids_f", [P, PICKS])
        layer_off = sb("layer_off", [P, DEPTH])
        stage_ids = sb("stage_ids", [P, R], U32)
        dots = sb("dots", [P, R])
        gel = sb("gel", [P, R])
        coef = sb("coef", [P, R])
        diag = sb("diag", [P, 2, P])
        zero_bf = sb("zero_bf", [32, SEQ], BF16)

        lat = scr[:, 3, 0:QR + KR]
        latT = scr[:, 5, 0:3 * P].rearrange("p (a n) -> p a n", n=P)
        sc = scr[:, 0:2, :]
        pr = scr[:, 2:4, :]
        pt = scr[:, 4:6, :]
        q_rows = scr[:, 0, 0:(MH + 1) * MD].rearrange("p (h d) -> p h d", d=MD)
        rope_a = scr[:, 1, 0:(MH + 1) * ROPE].rearrange("p (h k d) -> p h k d", h=MH + 1, k=2)
        rope_b = scr[:, 1, 256:256 + (MH + 1) * ROPE].rearrange("p (h k d) -> p h k d", h=MH + 1, k=2)
        k_rows = scr[:, 2, 0:MH * MD].rearrange("p (h d) -> p h d", d=MD)
        key_s = scr[:, 0:2, :].rearrange("p a (b k) -> p (a b) k", k=NK)
        cand = scr[:, 2:4, :].rearrange("p a (b k) -> p (a b) k", k=TOPK * TOPK)
        qT_peer = scr[:, 4:6, :].rearrange("p a (b k) -> p (a b) k", k=P)

        ident = consts[:, K_ID:K_ID + P]
        low_tri = consts[:, K_LT:K_LT + P]
        iota16 = consts[:, K_IOTA:K_IOTA + TOPK]

        acc = ctx.enter_context(nc.psum_tensor("acc", [P, D], F32))
        pa = ctx.enter_context(nc.psum_tensor("pa", [P, 2, SEQ], F32))
        pb = ctx.enter_context(nc.psum_tensor("pb", [P, 2, SEQ], F32))
        yp = ctx.enter_context(nc.psum_tensor("yp", [P, D], F32))

        s_load = sem("s_load")
        s_zero = sem("s_zero")
        s_w = [sem(f"s_w{i}") for i in range(WSLOTS)]
        s_wkf = sem("s_wkf")
        s_w_free = sem("s_w_free")
        s_wkf_free = sem("s_wkf_free")
        pa_full, pb_full, py_full = sem("pa_full"), sem("pb_full"), sem("py_full")
        pa_free = {e: sem(f"pa_free_{e}") for e in "av"}
        pb_free = {e: sem(f"pb_free_{e}") for e in "av"}
        py_free = {e: sem(f"py_free_{e}") for e in "av"}
        s_dve, s_act = sem("s_dve"), sem("s_act")
        s_past = {e: sem(f"s_past_{e}") for e in ("pe", "act", "dve", "pool")}
        s_ss = sem("s_ss")
        s_ln = sem("s_ln")
        s_var = sem("s_var")
        s_h = sem("s_h")
        s_fz = sem("s_fz")
        s_fl = sem("s_fl")
        s_logf = sem("s_logf")
        s_ccur = sem("s_ccur")
        s_ncT = sem("s_ncT")
        s_hT = sem("s_hT")
        s_gT = sem("s_gT")
        s_latT = sem("s_latT")
        s_qr = sem("s_qr")
        s_kr = sem("s_kr")
        s_knope = sem("s_knope")
        s_qk = sem("s_qk")
        s_mask = sem("s_mask")
        s_sc = sem("s_sc")
        s_sp = sem("s_sp")
        s_arg = sem("s_arg")
        s_p = sem("s_p")
        s_pt = sem("s_pt")
        s_pread = sem("s_pread")
        s_pv = sem("s_pv")
        s_y = sem("s_y")
        s_peerq = sem("s_peerq")
        s_keys = sem("s_keys")
        s_keysfree = sem("s_keysfree")
        s_best = sem("s_best")
        s_bexp = sem("s_bexp")
        s_ids = sem("s_ids")
        s_stage = sem("s_stage")
        s_u = [sem(f"s_u{i}") for i in range(R)]
        s_v = [sem(f"s_v{i}") for i in range(R)]
        s_dot = sem("s_dot")
        s_mm = sem("s_mm")
        s_gel = sem("s_gel")
        s_coef = sem("s_coef")
        s_diag = sem("s_diag")
        s_acc = sem("s_acc")
        s_acc_free = sem("s_acc_free")
        s_fin = sem("s_fin")
        s_out = sem("s_out")

        block = ctx.enter_context(nc.Block())

        def bc(ap2, axis, count):
            return ap2.unsqueeze(axis).to_broadcast(
                [*ap2.shape[:axis], count, *ap2.shape[axis:]])

        LOADS = []

        @block.sync
        def _(sp):
            def load(dst, src):
                sp.dma_start(dst, src).then_inc(s_load, 16)
                LOADS.append(1)

            load(x_all[:], x_d.rearrange("b (t p) d -> p (b t) d", p=P))
            load(consts[:], consts_d)
            load(gT_attn[:], attn_gT)
            load(gT_out[:], out_gT)
            load(gT_lat[:], lat_gT)
            load(w_uq_sb[:], w_uq.rearrange("l (c p) n -> p l c n", p=P))
            load(w_ukv_sb[:], w_ukv.rearrange("l p n -> p l n"))
            load(keys_sb[:], keys_T)
            load(gate_b[:], fgate_b.rearrange("l n -> (l n)").unsqueeze(0).to_broadcast([P, DEPTH * FH])
                 .rearrange("p (l n) -> p l n", l=DEPTH))
            load(ffn_gain[:], ffn_g.rearrange("l n -> (l n)").unsqueeze(0).to_broadcast([P, DEPTH * D])
                 .rearrange("p (l n) -> p l n", l=DEPTH))
            with sp.Fori(0, STEPS) as n:
                layer = n // TILES
                for i, (m, c, w) in enumerate(BLOCKS):
                    sp.wait_ge(s_w_free, n * NB + i + 1)
                    src = {"in": w_in, "out": w_out, "q": w_q}[m]
                    sp.dma_start(w_ring[:, i % WSLOTS, :, 0:w],
                                 src[bass.ds(layer, 1), :, c:c + w].rearrange("l (c p) n -> p (l c) n", p=P)
                                 ).then_inc(s_w[i % WSLOTS], 16)
                    if i == 0:
                        sp.wait_ge(s_wkf_free, n + 1)
                        sp.dma_start(w_kf[:, :, 0:ROPE],
                                     w_in[bass.ds(layer, 1), :, C_KR:C_KR + ROPE]
                                     .rearrange("l (c p) n -> p (l c) n", p=P)).then_inc(s_wkf, 16)
                        sp.dma_start(w_kf[:, :, ROPE:ROPE + FH],
                                     w_in[bass.ds(layer, 1), :, C_FL:C_FL + FH]
                                     .rearrange("l (c p) n -> p (l c) n", p=P)).then_inc(s_wkf, 16)
            sp.wait_ge(s_ids, STEPS)
            sp.dma_start(ffn_gain[:, 0, :], final_g.unsqueeze(0).to_broadcast([P, D])).then_inc(s_load, 16)
            for t in range(TILES):
                sp.wait_ge(s_fin, t + 1)
                sp.dma_start(out_d[0, t * P:(t + 1) * P, :], x_all[:, t, :]).then_inc(s_out, 16)
            sp.wait_ge(s_out, 16 * TILES)

        NLOADS = 16 * len(LOADS)

        @block.gpsimd
        def _(pool):
            for b in (kT_fox, kT_sb, kT_mla, v_fox, v_sb, v_mla, c_all, ncT, zero_bf):
                nc.gpsimd.memset(b[:], 0.0).then_inc(s_zero, 1)
            for l in range(DEPTH):
                nc.gpsimd.memset(layer_off[:, l:l + 1], float(l * EXPERTS)).then_inc(s_zero, 1)
            with pool.Fori(0, STEPS) as n:
                pool.wait_ge(s_ids, n + 1)
                pool.sem_inc(s_past["pool"], 1)
                with pool.Fori(0, ITS) as it:
                    for g in range(GPI):
                        pool.wait_ge(s_dot, n * PICKS + it * R + (g + 1) * G)
                        pool.wait_ge(s_mm, n * PICKS + it * R + (g + 1) * G)
                        nc.gpsimd.tensor_copy(stage_ids[:, g * G:g * G + G], ids[:, bass.ds(it * R + g * G, G)]
                                              ).then_inc(s_stage, 1)
                        pool.wait_ge(s_stage, n * ITS * GPI + it * GPI + g + 1)
                        pool.sem_inc(s_past["pool"], 1)
                        for j in range(g * G, g * G + G):
                            idx = bass.IndirectOffsetOnAxis(ap=stage_ids[:, j:j + 1], axis=0)
                            pool.indirect_dma_start(out=u_ring[:, j, :], out_offset=None, in_=u_d,
                                                    in_offset=idx).then_inc(s_u[j], 16)
                            pool.indirect_dma_start(out=v_ring[:, j, :], out_offset=None, in_=v_d,
                                                    in_offset=idx).then_inc(s_v[j], 16)

        @block.tensor
        def _(pe):
            def fill(n, ring, name, sems, label):
                b = ring.before(n, label)
                if b is not None:
                    pe.wait_ge(sems[b[0]], b[1])

            def past():
                pe.sem_inc(s_past["pe"], 1)

            def transposes(n, label, srcs, rows=P):
                fill(n, PB, "pb", pb_free, label)
                past()
                for i, s in enumerate(srcs):
                    mm = nc.tensor.transpose(pb[0:rows, PB.slot(label), i * P:(i + 1) * P], s, ident)
                return mm

            def weights(n, i):
                pe.wait_ge(s_w[i % WSLOTS], (n * (NB // WSLOTS) + i // WSLOTS + 1) * 16)

            def cols_T(n, i, label):
                w = BLOCKS[i][2]
                weights(n, i)
                fill(n, PA, "pa", pa_free, label)
                past()
                for j in range(w // P):
                    for c in range(KC):
                        mm = nc.tensor.matmul(pa[:, PA.slot(label), j * P:(j + 1) * P],
                                              w_ring[:, i % WSLOTS, c, j * P:(j + 1) * P], hT[:, c, :],
                                              start=(c == 0), stop=(c == KC - 1))
                mm.then_inc(pa_full, 1)
                pe.wait_ge(pa_full, PA.full(n, label))
                pe.sem_inc(s_w_free, 1)

            def rows_of(n, i, label):
                w = BLOCKS[i][2]
                weights(n, i)
                fill(n, PA, "pa", pa_free, label)
                past()
                for c in range(KC):
                    mm = nc.tensor.matmul(pa[:, PA.slot(label), 0:w], hT[:, c, :], w_ring[:, i % WSLOTS, c, 0:w],
                                          start=(c == 0), stop=(c == KC - 1))
                mm.then_inc(pa_full, 1)
                pe.wait_ge(pa_full, PA.full(n, label))
                pe.sem_inc(s_w_free, 1)

            def mixer(n):
                tile, layer = n % TILES, n // TILES
                pe.wait_ge(s_h, 4 * n + 1)
                for j in range(2):
                    transposes(n, f"hT{j}", [h[:, (4 * j + i) * P:(4 * j + i + 1) * P] for i in range(4)]
                               ).then_inc(pb_full, 1)
                pe.wait_ge(s_hT, 4 * n + 2)
                cols_T(n, 0, "fq")
                cols_T(n, 1, "fk")
                rows_of(n, 2, "fv")
                rows_of(n, 3, "cc")
                pe.wait_ge(s_wkf, 32 * (n + 1))
                fill(n, PA, "pa", pa_free, "kf")
                past()
                for c in range(KC):
                    mm = nc.tensor.matmul(pa[:, PA.slot("kf"), 0:ROPE + FH], hT[:, c, :], w_kf[:, c, :],
                                          start=(c == 0), stop=(c == KC - 1))
                mm.then_inc(pa_full, 1)
                pe.wait_ge(pa_full, PA.full(n, "kf"))
                pe.sem_inc(s_wkf_free, 1)
                cols_T(n, 4, "sq")
                cols_T(n, 5, "sk")
                rows_of(n, 6, "sv")
                pe.wait_ge(s_logf, n + 1)
                fill(n, PA, "pa", pa_free, "cum")
                past()
                nc.tensor.matmul(pa[:, PA.slot("cum"), 0:FH], low_tri, fl[:, 3, :], start=True, stop=False)
                nc.tensor.matmul(pa[:, PA.slot("cum"), 0:FH], ident[:, P - 1:P].to_broadcast([P, P]),
                                 c_all[:, bass.ds(tile, 1), :].rearrange("p a n -> p (a n)"),
                                 start=False, stop=True).then_inc(pa_full, 1)
                pe.wait_ge(s_ccur, n + 1)
                transposes(n, "ncT", [c_cur[:]], rows=FH).then_inc(pb_full, 1)
                pe.wait_ge(s_h, 4 * n + 2)
                transposes(n, "cqT", [lat[:, i * P:(i + 1) * P] for i in range(3)]).then_inc(pb_full, 1)
                pe.wait_ge(s_latT, n + 1)
                fill(n, PA, "pa", pa_free, "qup")
                past()
                for c in range(2):
                    mm = nc.tensor.matmul(pa[:, PA.slot("qup"), 0:MH * MD], latT[:, c, :],
                                          w_uq_sb[:, bass.ds(layer, 1), c, :].rearrange("p a n -> p (a n)"),
                                          start=(c == 0), stop=(c == 1))
                mm.then_inc(pa_full, 1)
                fill(n, PA, "pa", pa_free, "kvup")
                past()
                nc.tensor.matmul(pa[:, PA.slot("kvup"), :], latT[:, 2, :],
                                 w_ukv_sb[:, bass.ds(layer, 1), :].rearrange("p a n -> p (a n)"),
                                 start=True, stop=True).then_inc(pa_full, 1)
                pe.wait_ge(s_qr, n + 1)
                transposes(n, "qTm", [q_rows[:, i, :] for i in range(MH)], rows=MD).then_inc(pb_full, 1)
                pe.wait_ge(s_kr, n + 1)
                pe.wait_ge(s_knope, n + 1)
                transposes(n, "kTm", [k_rows[:, i, :] for i in range(MH)], rows=MD).then_inc(pb_full, 1)
                pe.wait_ge(s_ncT, n + 1)
                pe.wait_ge(s_qk, n + 1)

            def scores(n, i):
                lab = f"s{i}"
                fill(n, PA, "pa", pa_free, lab)
                past()
                o = pa[:, PA.slot(lab), :]
                if i < FH:
                    r = slice(64 * (i % 2), 64 * (i % 2) + 64)
                    nc.tensor.matmul(o, qT_fox[r, i // 2, :], kT_fox[r, i // 2, :], start=True, stop=False)
                    mm = nc.tensor.matmul(o, ident[0:FH, i:i + 1].to_broadcast([FH, P]), ncT[:, :],
                                          start=False, stop=True)
                elif i < FH + MH:
                    mm = nc.tensor.matmul(o, qT_mla[:, i - FH, :], kT_mla[:, i - FH, :], start=True, stop=True)
                else:
                    k = i - FH - MH
                    r = slice(64 * (k % 2), 64 * (k % 2) + 64)
                    mm = nc.tensor.matmul(o, qT_sb[r, k // 2, :], kT_sb[r, k // 2, :], start=True, stop=True)
                mm.then_inc(pa_full, 1)

            def turn(n, i):
                pe.wait_ge(s_p, n * HEADS + i + 1)
                transposes(n, f"p{i}", [pr[:, i % 2, b * P:(b + 1) * P] for b in range(TILES)]
                           ).then_inc(pb_full, 1)

            def pv(n, i):
                pe.wait_ge(s_pt, n * HEADS + i + 1)
                past()
                for b in range(TILES):
                    if i < FH:
                        v = v_fox[:, b, i * HD:(i + 1) * HD]
                    elif i < FH + MH:
                        v = v_mla[:, b, (i - FH) * HD:(i - FH + 1) * HD]
                    else:
                        v = v_sb[:, b, (i - FH - MH) * HD:(i - FH - MH + 1) * HD]
                    mm = nc.tensor.matmul(yp[:, i * HD:(i + 1) * HD], pt[:, i % 2, b * P:(b + 1) * P], v,
                                          start=(b == 0), stop=(b == TILES - 1))
                mm.then_inc(s_pv, 1)
                if i == HEADS - 1:
                    pe.wait_ge(s_pv, (n + 1) * HEADS)
                    pe.sem_inc(py_full, 1)

            def attention(n):
                for i in range(HEADS + 2):
                    if i < HEADS:
                        scores(n, i)
                    if 1 <= i <= HEADS:
                        turn(n, i - 1)
                    if i >= 2:
                        pv(n, i - 2)

            def output(n):
                pe.wait_ge(s_h, 4 * n + 3)
                for j in range(2):
                    transposes(n, f"yT{j}", [h[:, (4 * j + i) * P:(4 * j + i + 1) * P] for i in range(4)]
                               ).then_inc(pb_full, 1)
                pe.wait_ge(s_hT, 4 * n + 4)
                for j in range(3):
                    rows_of(n, 7 + j, f"wo{j}")

            def routing(n):
                layer = n // TILES
                pe.wait_ge(s_h, 4 * n + 4)
                for j in range(2):
                    transposes(n, f"gT{j}", [h[:, (4 * j + i) * P:(4 * j + i + 1) * P] for i in range(4)]
                               ).then_inc(pb_full, 1)
                pe.wait_ge(s_gT, 2 * n + 2)
                for g in range(2):
                    for j in range(3):
                        cols_T(n, 10 + 3 * g + j, f"wq{3 * g + j}")
                    pe.wait_ge(s_peerq, 6 * n + 3 * g + 3)
                    fill(n, PY, "py", py_free, f"ks{g}")
                    past()
                    for k in range(8):
                        mm = nc.tensor.matmul(yp[:, k * NK:(k + 1) * NK], qT_peer[:, k, :],
                                              keys_sb[:, bass.ds(layer, 1), k % 2, :].rearrange("p a n -> p (a n)"),
                                              start=True, stop=True)
                    mm.then_inc(py_full, 1)
                for ring, sems in ((PA, pa_free), (PB, pb_free), (PY, py_free)):
                    for e in "av":
                        pe.wait_ge(sems[e], (n + 1) * ring.per[e])

            def gather(n):
                pe.wait_ge(s_acc_free, n + 1)
                past()
                for c in range(2):
                    nc.tensor.matmul(acc[:, c * 512:c * 512 + 512], zero_bf[:, 0:P], zero_bf[:, :],
                                     start=True, stop=False)
                with pe.Fori(0, ITS) as it:
                    for j in range(R):
                        pe.wait_ge(s_diag, n * PICKS + it * R + j + 1)
                        pe.wait_ge(s_v[j], (n * ITS + it + 1) * 16)
                        for c in range(2):
                            mm = nc.tensor.matmul(acc[:, c * 512:c * 512 + 512], diag[:, j % 2, :],
                                                  v_ring[:, j, c * 512:c * 512 + 512], start=False, stop=False)
                        mm.then_inc(s_mm, 1)
                for c in range(2):
                    mm = nc.tensor.matmul(acc[:, c * 512:c * 512 + 512], zero_bf[:, 0:P], zero_bf[:, :],
                                          start=False, stop=True)
                mm.then_inc(s_acc, 1)

            pe.wait_ge(s_load, NLOADS)
            pe.wait_ge(s_zero, 9 + DEPTH)
            pe.sem_inc(s_w_free, WSLOTS)
            pe.sem_inc(s_wkf_free, 1)
            pe.sem_inc(s_mm, R)
            with pe.Fori(0, STEPS) as n:
                mixer(n)
                attention(n)
                output(n)
                routing(n)
                gather(n)

        @block.scalar
        def _(act):
            links = [0]

            def link(n, ins):
                links[0] += 1
                ins.then_inc(s_act, 1)
                act.wait_ge(s_act, n * ACT_LINKS + links[0])

            def past():
                act.sem_inc(s_past["act"], 1)

            def take(n, ring, full, label):
                act.wait_ge(full, ring.full(n, label))
                past()

            def squares(src, dst, junk):
                return nc.scalar.activation(junk, src, ACT.Square, accum_out=dst)

            def rsqrt(n, k, cols, dst):
                act.wait_ge(s_var, 4 * n + k)
                link(n, nc.scalar.activation(dst, cols, ACT.Ln))
                nc.scalar.activation(dst, dst, ACT.Exp, scale=-0.5).then_inc(s_ln, 1)

            def mixer(n):
                tile, layer = n % TILES, n // TILES
                act.wait_ge(s_acc_free, n + 1) if SEQUENTIAL else None
                past()
                squares(x_all[:, bass.ds(tile, 1), :].rearrange("p a n -> p (a n)"), stat[:, 0:1],
                        scr[:, 4:6, :].rearrange("p a n -> p (a n)")).then_inc(s_ss, 1)
                rsqrt(n, 1, stat[:, 4:5], stat[:, 8:9])
                past()
                nc.scalar.copy(mask[:], consts[:, bass.ds(K_MASK + (TILES - 1 - tile) * P, SEQ + 1)]).then_inc(s_mask, 1)
                take(n, PA, pa_full, "fq")
                nc.scalar.activation(qT_fox[:].rearrange("p a n -> p (a n)"), pa[:, PA.slot("fq"), 0:FW], ACT.Copy,
                                     scale=HD ** -0.5).then_inc(pa_free["a"], 1)
                take(n, PA, pa_full, "fk")
                nc.scalar.copy(kT_fox[:, :, bass.ds(tile * P, P)],
                               pa[:, PA.slot("fk"), 0:FW].rearrange("p (a n) -> p a n", n=P)).then_inc(pa_free["a"], 1)
                take(n, PA, pa_full, "fv")
                nc.scalar.copy(v_fox[:, bass.ds(tile, 1), :].rearrange("p a n -> p (a n)"),
                               pa[:, PA.slot("fv"), 0:FW]).then_inc(pa_free["a"], 1)
                act.wait_ge(s_fz, n + 1)
                link(n, nc.scalar.activation(fl[:, 1, :], fl[:, 0, :], ACT.Abs))
                link(n, nc.scalar.activation(fl[:, 1, :], fl[:, 1, :], ACT.Exp, scale=-1.0))
                nc.scalar.activation(fl[:, 1, :], fl[:, 1, :], ACT.Ln, bias=1.0).then_inc(s_fl, 1)
                link(n, squares(lat[:, 0:QR], stat[:, 1:2], scr[:, 4, 0:QR]))
                squares(lat[:, QR:QR + KR], stat[:, 2:3], scr[:, 4, 256:256 + KR]).then_inc(s_ss, 1)
                rsqrt(n, 2, stat[:, 5:7], stat[:, 9:11])
                take(n, PA, pa_full, "sq")
                nc.scalar.activation(qT_sb[:].rearrange("p a n -> p (a n)"), pa[:, PA.slot("sq"), 0:SW], ACT.Copy,
                                     scale=HD ** -0.5).then_inc(pa_free["a"], 1)
                take(n, PA, pa_full, "sk")
                nc.scalar.copy(kT_sb[:, :, bass.ds(tile * P, P)],
                               pa[:, PA.slot("sk"), 0:SW].rearrange("p (a n) -> p a n", n=P)).then_inc(pa_free["a"], 1)
                take(n, PA, pa_full, "sv")
                nc.scalar.copy(v_sb[:, bass.ds(tile, 1), :].rearrange("p a n -> p (a n)"),
                               pa[:, PA.slot("sv"), 0:SW]).then_inc(pa_free["a"], 1)
                take(n, PA, pa_full, "kvup")
                kv = pa[:, PA.slot("kvup"), :].rearrange("p (h d) -> p h d", d=2 * HD)
                nc.scalar.copy(k_rows[:, :, 0:NOPE], kv[:, :, 0:NOPE]).then_inc(s_knope, 1)
                nc.scalar.copy(v_mla[:, bass.ds(tile, 1), :].rearrange("p a (h d) -> p (a h) d", d=HD),
                               kv[:, :, NOPE:2 * HD]).then_inc(pa_free["a"], 1)
                take(n, PB, pb_full, "qTm")
                nc.scalar.activation(qT_mla[:].rearrange("p a n -> p (a n)"), pb[0:MD, PB.slot("qTm"), :], ACT.Copy,
                                     scale=MD ** -0.5).then_inc(pb_free["a"], 1)
                take(n, PB, pb_full, "kTm")
                nc.scalar.copy(kT_mla[:, :, bass.ds(tile * P, P)],
                               pb[0:MD, PB.slot("kTm"), :].rearrange("p (a n) -> p a n", n=P)
                               ).then_inc(pb_free["a"], 1)
                act.wait_ge(pa_free["a"], n * PA.per["a"] + 7)
                act.wait_ge(pb_free["a"], n * PB.per["a"] + 2)
                act.sem_inc(s_qk, 1)

            def first(n, i):
                act.wait_ge(s_sc, n * HEADS + i + 1)
                past()
                if i >= 2:
                    act.wait_ge(s_pread, n * HEADS + i - 1)
                    past()
                s, p = sc[:, i % 2, :], pr[:, i % 2, :]
                if i < FH + MH:
                    nc.scalar.activation(p, s, ACT.Exp, scale=-1.0, bias=nmax[:, i:i + 1],
                                         accum_out=rsum[:, i:i + 1]).then_inc(s_p, 1)
                else:
                    link(n, nc.scalar.activation(p, s, ACT.Abs))
                    link(n, nc.scalar.activation(p, p, ACT.Exp, scale=-1.0))
                    nc.scalar.activation(p, p, ACT.Ln, bias=1.0).then_inc(s_sp, 1)

            def second(n, i):
                if i >= FH + MH:
                    act.wait_ge(s_arg, n * SH + i - FH - MH + 1)
                    nc.scalar.activation(pr[:, i % 2, :], pr[:, i % 2, :], ACT.Exp).then_inc(s_p, 1)

            def turned(n, i):
                take(n, PB, pb_full, f"p{i}")
                if i >= 2:
                    act.wait_ge(s_pv, n * HEADS + i - 1)
                    past()
                nc.scalar.copy(pt[:, i % 2, :], pb[:, PB.slot(f"p{i}"), :]).then_inc(s_pt, 1)
                act.wait_ge(s_pt, n * HEADS + i + 1)
                act.sem_inc(pb_free["a"], 1)
                act.sem_inc(s_pread, 1)

            def attention(n):
                for i in range(HEADS + 2):
                    if i < HEADS:
                        first(n, i)
                    if 1 <= i <= HEADS:
                        second(n, i - 1)
                    if i >= 2 - 1 and i - 1 < HEADS:
                        turned(n, i - 1)

            def output(n):
                act.wait_ge(s_y, n + 1)
                past()
                for k, (a, b) in enumerate(((0, FW), (FW, FW + MW), (FW + MW, D))):
                    link(n, squares(h[:, a:b], stat[:, 12 + k:13 + k], scr[:, 0:2, :].rearrange("p a n -> p (a n)")[:, a:b]))
                act.sem_inc(s_ss, 1)
                rsqrt(n, 3, stat[:, 16:19], stat[:, 20:23])
                act.wait_ge(pa_free["v"], n * PA.per["v"] + PA.per["v"])
                past()
                squares(x_all[:, bass.ds(n % TILES, 1), :].rearrange("p a n -> p (a n)"), stat[:, 0:1],
                        scr[:, 4:6, :].rearrange("p a n -> p (a n)")).then_inc(s_ss, 1)
                rsqrt(n, 4, stat[:, 4:5], stat[:, 8:9])

            def routing(n):
                for j in range(2):
                    take(n, PB, pb_full, f"gT{j}")
                    nc.scalar.copy(hT[:, 4 * j:4 * j + 4, :].rearrange("p a n -> p (a n)"), pb[:, PB.slot(f"gT{j}"), :]
                                   ).then_inc(s_gT, 1)
                    act.wait_ge(s_gT, 2 * n + j + 1)
                    act.sem_inc(pb_free["a"], 1)
                for g in range(2):
                    for j in range(3):
                        i = 3 * g + j
                        w = BLOCKS[10 + i][2]
                        take(n, PA, pa_full, f"wq{i}")
                        if g == 1 and j == 0:
                            act.wait_ge(py_full, PY.full(n, "ks0"))
                            past()
                        nc.scalar.copy(qT_peer[:, 3 * j:3 * j + w // P, :].rearrange("p a n -> p (a n)"),
                                       pa[:, PA.slot(f"wq{i}"), 0:w]).then_inc(s_peerq, 1)
                        act.wait_ge(s_peerq, 6 * n + i + 1)
                        act.sem_inc(pa_free["a"], 1)
                    take(n, PY, py_full, f"ks{g}")
                    if g == 1:
                        act.wait_ge(s_keysfree, 2 * n + 1)
                        past()
                    for j in range(2):
                        ins = nc.scalar.copy(key_s[:, 4 * j:4 * j + 4, :].rearrange("p a n -> p (a n)"),
                                             yp[:, j * 512:j * 512 + 512])
                        link(n, ins)
                    act.sem_inc(s_keys, 1)
                    act.sem_inc(py_free["a"], 1)
                act.wait_ge(s_best, n + 1)
                nc.scalar.activation(best[:], best[:], ACT.Exp).then_inc(s_bexp, 1)

            def gather(n):
                with act.Fori(0, ITS) as it:
                    for q in range(GPI):
                        act.wait_ge(s_dot, n * PICKS + it * R + (q + 1) * G + R)
                        nc.scalar.activation(gel[:, q * G:q * G + G], dots[:, q * G:q * G + G], ACT.Gelu
                                             ).then_inc(s_gel, 1)
                        act.wait_ge(s_gel, (n * ITS + it) * GPI + q + 1 + GPI)
                        past()
                        for j in range(q * G, q * G + G):
                            ins = nc.scalar.activation(coef[:, j:j + 1], gel[:, j:j + 1], ACT.Copy,
                                                       scale=gates[:, bass.ds(it * R + j, 1)])
                        ins.then_inc(s_coef, 1)
                        act.wait_ge(s_coef, (n * ITS + it) * GPI + q + 1)
                        for j in range(q * G, q * G + G):
                            act.wait_ge(s_mm, n * PICKS + it * R + j - 1 + R)
                            nc.scalar.activation(diag[:, j % 2, :], ident, ACT.Copy, scale=coef[:, j:j + 1]
                                                 ).then_inc(s_diag, 1)

            act.wait_ge(s_load, NLOADS)
            act.wait_ge(s_zero, 9 + DEPTH)
            with act.Fori(0, STEPS) as n:
                mixer(n)
                attention(n)
                output(n)
                routing(n)
                act.wait_ge(s_ids, n + 1)
                past()
                gather(n)
            assert links[0] == ACT_LINKS, links
            act.wait_ge(s_acc_free, STEPS + 1)
            spare = [h[:], h_dot[:]] + [scr[:, k:k + 2, :].rearrange("p a n -> p (a n)") for k in (2, 4)]
            for t in range(TILES):
                squares(x_all[:, t, :], stat[:, 24 + t:25 + t], spare[t]).then_inc(s_ss, 1)
            act.wait_ge(s_var, 4 * STEPS + 1)
            nc.scalar.activation(stat[:, 8:12], stat[:, 4:8], ACT.Ln).then_inc(s_act, 1)
            act.wait_ge(s_act, STEPS * ACT_LINKS + 1)
            nc.scalar.activation(stat[:, 8:12], stat[:, 8:12], ACT.Exp, scale=-0.5).then_inc(s_ln, 1)

        @block.vector
        def _(dve):
            links = [0]

            def link(n, ins):
                links[0] += 1
                ins.then_inc(s_dve, 1)
                dve.wait_ge(s_dve, n * DVE_LINKS + links[0])

            def past():
                dve.sem_inc(s_past["dve"], 1)

            def take(n, ring, full, label):
                dve.wait_ge(full, ring.full(n, label))
                past()

            def refine(n, k, var, est, dst, tmp):
                dve.wait_ge(s_ln, 4 * n + k)
                link(n, nc.vector.tensor_tensor(tmp, est, est, ALU.mult))
                link(n, nc.vector.tensor_tensor(tmp, tmp, var, ALU.mult))
                link(n, nc.vector.tensor_scalar(tmp, tmp, -0.5, 1.5, ALU.mult, ALU.add))
                link(n, nc.vector.tensor_tensor(dst, est, tmp, ALU.mult))

            def variance(dst, src, width):
                return nc.vector.tensor_scalar(dst, src, 1.0 / width, EPS, ALU.mult, ALU.add)

            def x_tile(n):
                return x_all[:, bass.ds(n % TILES, 1), :].rearrange("p a n -> p (a n)")

            def mixer(n):
                tile, layer = n % TILES, n // TILES
                dve.wait_ge(s_ss, 4 * n + 1)
                variance(stat[:, 4:5], stat[:, 0:1], D).then_inc(s_var, 1)
                refine(n, 1, stat[:, 4:5], stat[:, 8:9], stat[:, 30:31], stat[:, 31:32])
                past()
                nc.vector.tensor_scalar(h[:], x_tile(n), stat[:, 30:31], None, ALU.mult).then_inc(s_h, 1)

                def turned(labels, gT):
                    for j, lab in enumerate(labels):
                        take(n, PB, pb_full, lab)
                        nc.vector.tensor_tensor(
                            hT[:, 4 * j:4 * j + 4, :], pb[:, PB.slot(lab), :].rearrange("p (a n) -> p a n", n=P),
                            bc(gT[:, bass.ds(layer, 1), 4 * j:4 * j + 4].rearrange("p a n -> p (a n)"), 2, P),
                            ALU.mult).then_inc(s_hT, 1)
                        dve.wait_ge(s_hT, 4 * n + j + (1 if gT is gT_attn else 3))
                        dve.sem_inc(pb_free["v"], 1)

                turned(["hT0", "hT1"], gT_attn)
                take(n, PA, pa_full, "cc")
                nc.vector.tensor_copy(lat, pa[:, PA.slot("cc"), 0:QR + KR]).then_inc(pa_free["v"], 1)
                take(n, PA, pa_full, "kf")
                nc.vector.tensor_copy(q_rows[:, MH, NOPE:MD], pa[:, PA.slot("kf"), 0:ROPE])
                nc.vector.tensor_tensor(fl[:, 0, :], pa[:, PA.slot("kf"), ROPE:ROPE + FH],
                                        gate_b[:, bass.ds(layer, 1), :].rearrange("p a n -> p (a n)"),
                                        ALU.add).then_inc(pa_free["v"], 1)
                dve.wait_ge(pa_free["v"], n * PA.per["v"] + 2)
                dve.sem_inc(s_fz, 1)
                dve.wait_ge(s_fl, n + 1)
                nc.vector.scalar_tensor_tensor(out=fl[:, 3, :], in0=fl[:, 0, :], scalar=0.0, in1=fl[:, 1, :],
                                               op0=ALU.min, op1=ALU.subtract).then_inc(s_logf, 1)
                dve.wait_ge(s_ss, 4 * n + 2)
                link(n, variance(stat[:, 5:6], stat[:, 1:2], QR))
                variance(stat[:, 6:7], stat[:, 2:3], KR).then_inc(s_var, 1)
                refine(n, 2, stat[:, 5:7], stat[:, 9:11], stat[:, 26:28], stat[:, 28:30])
                link(n, nc.vector.tensor_scalar(lat[:, 0:QR], lat[:, 0:QR], stat[:, 26:27], None, ALU.mult))
                nc.vector.tensor_scalar(lat[:, QR:], lat[:, QR:], stat[:, 27:28], None, ALU.mult).then_inc(s_h, 1)
                take(n, PA, pa_full, "cum")
                nc.vector.tensor_copy(c_cur[:], pa[:, PA.slot("cum"), 0:FH]).then_inc(s_ccur, 1)
                nc.vector.tensor_copy(c_all[:, bass.ds(tile + 1, 1), :].rearrange("p a n -> p (a n)"),
                                      pa[:, PA.slot("cum"), 0:FH]).then_inc(pa_free["v"], 1)
                take(n, PB, pb_full, "ncT")
                nc.vector.tensor_scalar(ncT[:, bass.ds(tile * P, P)], pb[0:FH, PB.slot("ncT"), 0:P], -1.0, None,
                                        ALU.mult).then_inc(s_ncT, 1)
                dve.wait_ge(s_ncT, n + 1)
                dve.sem_inc(pb_free["v"], 1)
                take(n, PB, pb_full, "cqT")
                nc.vector.tensor_tensor(
                    latT, pb[:, PB.slot("cqT"), 0:3 * P].rearrange("p (a n) -> p a n", n=P),
                    bc(gT_lat[:, bass.ds(layer, 1), :].rearrange("p a n -> p (a n)"), 2, P),
                    ALU.mult).then_inc(s_latT, 1)
                dve.wait_ge(s_latT, n + 1)
                dve.sem_inc(pb_free["v"], 1)
                take(n, PA, pa_full, "qup")
                nc.vector.tensor_copy(q_rows[:, 0:MH, :],
                                      pa[:, PA.slot("qup"), 0:MH * MD].rearrange("p (h d) -> p h d", d=MD)
                                      ).then_inc(pa_free["v"], 1)
                dve.wait_ge(pa_free["v"], n * PA.per["v"] + 4)
                hf = ROPE // 2
                rot = q_rows[:, :, NOPE:MD].rearrange("p h (k d) -> p h k d", k=2)
                past()
                for k in range(2):
                    t = consts[:, bass.ds(tile * ROPE + K_ROPE, hf)]
                    link(n, nc.vector.tensor_tensor(rope_a[:, :, k, :], rot[:, :, k, :], bc(t, 1, MH + 1), ALU.mult))
                    t = consts[:, bass.ds(tile * ROPE + K_ROPE + hf, hf)]
                    link(n, nc.vector.tensor_tensor(rope_b[:, :, k, :], rot[:, :, k, :], bc(t, 1, MH + 1), ALU.mult))
                link(n, nc.vector.tensor_tensor(rot[:, :, 0, :], rope_a[:, :, 0, :], rope_b[:, :, 1, :], ALU.subtract))
                link(n, nc.vector.tensor_tensor(rot[:, :, 1, :], rope_b[:, :, 0, :], rope_a[:, :, 1, :], ALU.add))
                dve.sem_inc(s_qr, 1)
                nc.vector.tensor_copy(k_rows[:, :, NOPE:MD],
                                      q_rows[:, MH:MH + 1, NOPE:MD].to_broadcast([P, MH, ROPE])).then_inc(s_kr, 1)
                dve.wait_ge(s_mask, n + 1)
                dve.wait_ge(s_qk, n + 1)
                past()

            def first(n, i):
                take(n, PA, pa_full, f"s{i}")
                if 2 <= i:
                    dve.wait_ge(s_p, n * HEADS + i - 1)
                    past()
                s, z = sc[:, i % 2, :], pa[:, PA.slot(f"s{i}"), :]
                if i < FH + MH:
                    nc.vector.tensor_tensor_reduce(s, z, mask[:, 0:SEQ], -1.0, -NEG, ALU.add, ALU.min,
                                                   nmax[:, i:i + 1]).then_inc(s_sc, 1)
                else:
                    nc.vector.tensor_tensor(s, z, mask[:, 1:SEQ + 1], ALU.add).then_inc(s_sc, 1)
                dve.wait_ge(s_sc, n * HEADS + i + 1)
                dve.sem_inc(pa_free["v"], 1)

            def second(n, i):
                k = i - FH - MH
                if k < 0:
                    return
                s, p = sc[:, i % 2, :], pr[:, i % 2, :]
                dve.wait_ge(s_sp, n * SH + k + 1)
                link(n, nc.vector.scalar_tensor_tensor(out=p, in0=s, scalar=0.0, in1=p, op0=ALU.max, op1=ALU.add))
                back = pr[:, i % 2, ::-1]
                link(n, nc.vector.tensor_tensor_scan(back, consts[:, K_LT + P - 1:K_LT + P].to_broadcast([P, SEQ]),
                                                     back, 0.0, ALU.mult, ALU.add))
                nc.vector.tensor_tensor(p, s, p, ALU.subtract).then_inc(s_arg, 1)

            def attention(n):
                for i in range(HEADS + 1):
                    if i < HEADS:
                        first(n, i)
                    if i >= 1:
                        second(n, i - 1)

            def output(n):
                layer = n // TILES
                dve.wait_ge(s_p, (n + 1) * HEADS)
                link(n, nc.vector.reciprocal(rinv[:, 0:FH + MH], rsum[:, 0:FH + MH]))
                take(n, PY, py_full, "y")
                link(n, nc.vector.tensor_tensor(
                    h[:, 0:FW + MW].rearrange("p (h d) -> p h d", d=HD),
                    yp[:, 0:FW + MW].rearrange("p (h d) -> p h d", d=HD),
                    bc(rinv[:, 0:FH + MH], 2, HD), ALU.mult))
                link(n, nc.vector.tensor_copy(h[:, FW + MW:D], yp[:, FW + MW:D]))
                dve.sem_inc(s_y, 1)
                dve.sem_inc(py_free["v"], 1)
                dve.wait_ge(s_ss, 4 * n + 3)
                link(n, variance(stat[:, 16:17], stat[:, 12:13], FW))
                link(n, variance(stat[:, 17:18], stat[:, 13:14], MW))
                variance(stat[:, 18:19], stat[:, 14:15], SW).then_inc(s_var, 1)
                refine(n, 3, stat[:, 16:19], stat[:, 20:23], stat[:, 23:26], stat[:, 26:29])
                for k, (a, b) in enumerate(((0, FW), (FW, FW + MW), (FW + MW, D))):
                    ins = nc.vector.tensor_scalar(h[:, a:b], h[:, a:b], stat[:, 23 + k:24 + k], None, ALU.mult)
                    if k == 2:
                        ins.then_inc(s_h, 1)
                    else:
                        link(n, ins)
                for j in range(2):
                    lab = f"yT{j}"
                    take(n, PB, pb_full, lab)
                    nc.vector.tensor_tensor(
                        hT[:, 4 * j:4 * j + 4, :], pb[:, PB.slot(lab), :].rearrange("p (a n) -> p a n", n=P),
                        bc(gT_out[:, bass.ds(layer, 1), 4 * j:4 * j + 4].rearrange("p a n -> p (a n)"), 2, P),
                        ALU.mult).then_inc(s_hT, 1)
                    dve.wait_ge(s_hT, 4 * n + j + 3)
                    dve.sem_inc(pb_free["v"], 1)
                for j in range(3):
                    i = 7 + j
                    c, w = BLOCKS[i][1], BLOCKS[i][2]
                    take(n, PA, pa_full, f"wo{j}")
                    xs = x_all[:, bass.ds(n % TILES, 1), c:c + w].rearrange("p a n -> p (a n)")
                    nc.vector.tensor_tensor(xs, xs, pa[:, PA.slot(f"wo{j}"), 0:w], ALU.add).then_inc(pa_free["v"], 1)
                dve.wait_ge(s_ss, 4 * n + 4)
                variance(stat[:, 4:5], stat[:, 0:1], D).then_inc(s_var, 1)
                refine(n, 4, stat[:, 4:5], stat[:, 8:9], stat[:, 30:31], stat[:, 31:32])
                past()
                nc.vector.scalar_tensor_tensor(
                    out=h[:], in0=x_tile(n), scalar=stat[:, 30:31],
                    in1=ffn_gain[:, bass.ds(layer, 1), :].rearrange("p a n -> p (a n)"),
                    op0=ALU.mult, op1=ALU.mult).then_inc(s_h, 1)

            def best16(n, src, vals, idx):
                past()
                for a, b in ((0, 8), (8, 16)):
                    for s, v in zip(src, vals):
                        ins = nc.vector.max(v[:, a:b], s)
                    link(n, ins)
                    past()
                    for s, v, i in zip(src, vals, idx):
                        ins = nc.vector.max_index(i[:, a:b], v[:, a:b], s)
                    link(n, ins)
                    past()
                    if a == 0:
                        for s, v in zip(src, vals):
                            ins = nc.vector.match_replace(out=s, in_to_replace=v[:, a:b], in_values=s, imm_value=GONE)
                        link(n, ins)
                        past()

            def routing(n):
                layer = n // TILES
                for g in range(2):
                    dve.wait_ge(s_keys, 2 * n + g + 1)
                    best16(n, [key_s[:, k, :] for k in range(8)], [top[:, k, :] for k in range(8)],
                           [top_i[:, k, :] for k in range(8)])
                    link(n, nc.vector.tensor_copy(top_f[:], top_i[:]))
                    pair = top[:].rearrange("p (h k) n -> p h k n", k=2)
                    for j in range(4):
                        ins = nc.vector.tensor_tensor(cand[:, j, :].rearrange("p (a b) -> p a b", b=TOPK),
                                                bc(pair[:, j, 0, :], 2, TOPK), bc(pair[:, j, 1, :], 1, TOPK), ALU.add)
                    link(n, ins)
                    bs = best[:, 4 * g:4 * g + 4, :]
                    best16(n, [cand[:, j, :] for j in range(4)], [bs[:, j, :] for j in range(4)],
                           [pos[:, j, :] for j in range(4)])
                    flat = pos[:].rearrange("p a n -> p (a n)")
                    nc.vector.tensor_scalar(pos_h[:, 0, :], flat, 4, None, ALU.logical_shift_right)
                    link(n, nc.vector.tensor_scalar(pos_h[:, 1, :], flat, TOPK - 1, None, ALU.bitwise_and))
                    link(n, nc.vector.tensor_copy(pos_f[:], pos_h[:]))
                    for k in range(2):
                        hot = cand[:].rearrange("p a n -> p (a n)").rearrange("p (m i) -> p m i", i=TOPK)
                        link(n, nc.vector.tensor_tensor(hot, bc(pos_f[:, k, :], 2, TOPK),
                                                        bc(iota16, 1, 4 * TOPK), ALU.is_equal))
                        for j in range(4):
                            hj = cand[:, j, :].rearrange("p (m i) -> p m i", i=TOPK)
                            ins = nc.vector.tensor_tensor(hj, hj, bc(top_f[:, 2 * j + k, :], 1, TOPK), ALU.mult)
                        link(n, ins)
                        link(n, nc.vector.tensor_reduce(key_f[:, k, :], hot, AX.X, ALU.add))
                    dve.sem_inc(s_keysfree, 1)
                    link(n, nc.vector.scalar_tensor_tensor(out=ids_f[:, 64 * g:64 * g + 64], in0=key_f[:, 0, :],
                                                           scalar=float(NK), in1=key_f[:, 1, :],
                                                           op0=ALU.mult, op1=ALU.add))
                link(n, nc.vector.tensor_copy(gsum[:, 0, :], best[:, :, 0]))
                nc.vector.tensor_tensor(best[:], best[:], bc(gsum[:, 0, :], 2, TOPK), ALU.subtract).then_inc(s_best, 1)
                dve.wait_ge(s_bexp, n + 1)
                link(n, nc.vector.tensor_reduce(gsum[:, 0, :], best[:], AX.X, ALU.add))
                link(n, nc.vector.reciprocal(gsum[:, 1, :], gsum[:, 0, :]))

            def hand_over(n):
                layer = n // TILES
                dve.wait_ge(s_stage, n * ITS * GPI) if not SEQUENTIAL else None
                past()
                nc.vector.tensor_scalar(ids[:], ids_f[:], layer_off[:, bass.ds(layer, 1)], None, ALU.add)
                nc.vector.tensor_copy(h_dot[:], h[:])
                link(n, nc.vector.tensor_tensor(gates[:].rearrange("p (h n) -> p h n", n=TOPK), best[:],
                                                bc(gsum[:, 1, :], 2, TOPK), ALU.mult))
                dve.sem_inc(s_ids, 1)

            def gather(n):
                with dve.Fori(0, ITS) as it:
                    for j in range(R):
                        dve.wait_ge(s_u[j], (n * ITS + it + 1) * 16)
                        if j % G == 0:
                            dve.wait_ge(s_gel, (n * ITS + it) * GPI + j // G + 1)
                        nc.vector.tensor_tensor_reduce(u_ring[:, j, :], u_ring[:, j, :], h_dot[:], 1.0, 0.0,
                                                       ALU.mult, ALU.add, dots[:, j:j + 1]).then_inc(s_dot, 1)

            def add_experts(n):
                dve.wait_ge(s_acc, n + 1)
                past()
                nc.vector.tensor_tensor(x_tile(n), x_tile(n), acc[:], ALU.add).then_inc(s_acc_free, 1)

            dve.wait_ge(s_load, NLOADS)
            dve.wait_ge(s_zero, 9 + DEPTH)
            dve.sem_inc(s_dot, R)
            dve.sem_inc(s_gel, GPI)
            dve.sem_inc(s_acc_free, 1)
            with dve.Fori(0, STEPS) as n:
                mixer(n)
                attention(n)
                output(n)
                routing(n)
                hand_over(n)
                gather(n)
                add_experts(n)
            assert links[0] == DVE_LINKS, links
            base = STEPS * DVE_LINKS
            dve.wait_ge(s_ss, 4 * STEPS + TILES)
            variance(stat[:, 4:8], stat[:, 24:28], D).then_inc(s_var, 1)
            dve.wait_ge(s_ln, 4 * STEPS + 1)
            v, e, t, r = stat[:, 4:8], stat[:, 8:12], stat[:, 12:16], stat[:, 16:20]
            for k, f in enumerate((lambda: nc.vector.tensor_tensor(t, e, e, ALU.mult),
                                   lambda: nc.vector.tensor_tensor(t, t, v, ALU.mult),
                                   lambda: nc.vector.tensor_scalar(t, t, -0.5, 1.5, ALU.mult, ALU.add),
                                   lambda: nc.vector.tensor_tensor(r, e, t, ALU.mult))):
                f().then_inc(s_dve, 1)
                dve.wait_ge(s_dve, base + k + 1)
            dve.wait_ge(s_load, NLOADS + 16)
            for k in range(TILES):
                nc.vector.scalar_tensor_tensor(out=x_all[:, k, :], in0=x_all[:, k, :], scalar=stat[:, 16 + k:17 + k],
                                               in1=ffn_gain[:, 0, :], op0=ALU.mult, op1=ALU.mult).then_inc(s_fin, 1)


SEQUENTIAL = True


def shape_constants():
    k = np.zeros((P, KW), np.float32)
    k[:, K_ID:K_ID + P] = np.eye(P, dtype=np.float32)
    s = np.arange(897)[None, :] - (TILES - 1) * P
    k[:, K_MASK:K_MASK + 897] = np.where(s <= np.arange(P)[:, None], 0.0, NEG)
    k[:, K_LT:K_LT + P] = np.triu(np.ones((P, P), np.float32))
    k[:, K_IOTA:K_IOTA + TOPK] = np.arange(TOPK)
    half = ROPE // 2
    inv = (1.0 / (np.float32(10000.0) ** (np.arange(half, dtype=np.float32) / np.float32(half)))).astype(np.float32)
    ang = np.arange(SEQ, dtype=np.float32)[:, None] * inv[None, :]
    cs = np.concatenate([np.cos(ang), np.sin(ang)], axis=1).astype(np.float32)
    k[:, K_ROPE:] = cs.reshape(TILES, P, ROPE).transpose(1, 0, 2).reshape(P, TILES * ROPE)
    return k


def kernel(**inputs):
    import concourse.bacc as _bacc
    from concourse.bass_utils import run_bass_kernel_spmd as _run

    def parts(a):
        a = np.asarray(a)
        return np.ascontiguousarray(a.reshape(a.shape[0], -1, P).transpose(2, 0, 1))

    i = {k: np.asarray(v) for k, v in inputs.items()}
    data = {
        "x": i["x"], "w_in": i["w_in"], "fgate_b": i["fgate_b"], "attn_gT": parts(i["attn_norm_g"]),
        "lat_gT": parts(np.concatenate([i["mla_q_norm_g"], i["mla_kv_norm_g"]], axis=1)),
        "out_gT": parts(np.concatenate([i["out_norm_fox"], i["out_norm_mla"], i["out_norm_sb"]], axis=1)),
        "ffn_g": i["ffn_norm_g"], "final_g": i["final_norm_g"], "w_uq": i["w_uq"], "w_ukv": i["w_ukv"],
        "w_out": i["w_out"], "w_q": i["peer_w_query"],
        "keys_T": np.stack([i["peer_keys1"], i["peer_keys2"]], axis=1).transpose(3, 0, 1, 2),
        "u": i["peer_u"].reshape(DEPTH * EXPERTS, D), "v": i["peer_v"].reshape(DEPTH * EXPERTS, D),
        "consts": shape_constants(),
    }
    nc = _bacc.Bacc("TRN2", target_bir_lowering=False, num_devices=1)
    arrays, args = {}, []
    for name, a in data.items():
        a = np.ascontiguousarray(a)
        arrays[f"in_{name}_dram"] = a
        args.append(nc.dram_tensor(f"in_{name}_dram", a.shape, mybir.dt.from_np(a.dtype), kind="ExternalInput").ap())
    out = nc.dram_tensor("out_0_dram", (1, SEQ, D), F32, kind="ExternalOutput").ap()
    trunk(nc, *args, out)
    r = _run(nc, [arrays], core_ids=[0])
    return r.results[0]["out_0_dram"]
```

```python
from contextlib import ExitStack

import numpy as np

import concourse.bass as bass
from concourse import mybir

F32 = mybir.dt.float32
BF16 = mybir.dt.bfloat16
U32 = mybir.dt.uint32
ALU = mybir.AluOpType
ACT = mybir.ActivationFunctionType
AX = mybir.AxisListType

P = 128
D = 1024
SEQ = 512
DEPTH = 2
TILES = SEQ // P
STEPS = DEPTH * TILES
KC = D // P
HD = 64
FH, MH, SH = 6, 4, 6
HEADS = FH + MH + SH
FW, MW, SW = FH * HD, MH * HD, SH * HD
QR, KR = 256, 128
NOPE, ROPE = 64, 32
MD = NOPE + ROPE
EPS = 1e-6
NEG = -1e30
GONE = -3.0e38

PH = 8
NK = 128
TOPK = 16
EXPERTS = NK * NK
PICKS = PH * TOPK

C_FQ, C_FK, C_FV, C_FL = 0, FW, 2 * FW, 3 * FW
C_CQ = C_FL + FH
C_KR = C_CQ + QR + KR
C_SQ = C_KR + ROPE
C_SK, C_SV = C_SQ + SW, C_SQ + 2 * SW

WMAX = 384
BLOCKS = ([("in", c, WMAX) for c in (C_FQ, C_FK, C_FV, C_CQ, C_SQ, C_SK, C_SV)]
          + [("out", c, min(WMAX, D - c)) for c in range(0, D, WMAX)]
          + [("q", g * D + c, min(WMAX, D - c)) for g in range(2) for c in range(0, D, WMAX)])
NB = len(BLOCKS)
WSLOTS = 2
assert NB % WSLOTS == 0

K_ID, K_MASK, K_LT, K_IOTA, K_ROPE = 0, 128, 128 + 897, 256 + 897, 272 + 897
KW = K_ROPE + TILES * 2 * (ROPE // 2)


def FIRST(n):
    return isinstance(n, int) and n == 0


R = 8
G = 4
VE = 1
PE = G - VE
GROUPS = PICKS // G
ITS = GROUPS // 2

POINTS = (["norm", "fq", "fk", "fv", "cc", "sq", "sk", "sv", "lat", "kvup"]
          + [f"head{i}" for i in range(1, HEADS, 2)] + ["y", "wo", "ffn"]
          + ["g0a", "g0b", "g0c", "g0d", "g0e", "g1a", "g1b", "g1c", "g1d", "g1e", "end"])
assert len(POINTS) == GROUPS, len(POINTS)


class Places:

    def __init__(self):
        self.p = 0

    def next(self, label):
        assert POINTS[self.p % GROUPS] == label, (POINTS[self.p % GROUPS], label)
        self.p += 1
        return (self.p - 1) % GROUPS


class Ring:

    def __init__(self, bufs, fills):
        self.bufs = bufs
        self.labels = [x for x, _ in fills]
        self.by = [e for _, e in fills]
        self.per = {e: self.by.count(e) for e in "av"}

    def slot(self, label):
        return self.labels.index(label) % self.bufs

    def full(self, n, label):
        return n * len(self.labels) + self.labels.index(label) + 1

    def before(self, n, label):
        i = self.labels.index(label) - self.bufs
        if i < 0:
            return None
        e = self.by[i]
        return e, n * self.per[e] + self.by[:i].count(e) + 1


PA = Ring(2, [("fq", "a"), ("fk", "a"), ("fv", "a"), ("cc", "v"), ("kf", "v"), ("sq", "a"), ("sk", "a"),
              ("sv", "a"), ("cum", "v"), ("qup", "v"), ("kvup", "a")]
          + [(f"s{i}", "v") for i in range(HEADS)] + [(f"wo{i}", "v") for i in range(3)]
          + [(f"wq{i}", "a") for i in range(6)])
PB = Ring(2, [("hT0", "v"), ("hT1", "v"), ("ncT", "v"), ("cqT", "v"), ("qTm", "a"), ("kTm", "a")]
          + [(f"p{i}", "a") for i in range(HEADS)]
          + [("yT0", "v"), ("yT1", "v"), ("gT0", "a"), ("gT1", "a")])
PY = Ring(1, [("y", "v"), ("ks0", "a"), ("ks1", "a")])

DVE_LINKS = 89
ACT_LINKS = 26


def trunk(nc, x_d, w_in, fgate_b, attn_gT, lat_gT, out_gT, ffn_g, final_g, w_uq, w_ukv, w_out,
          w_q, keys_T, u_d, v_d, consts_d, out_d):
    with ExitStack() as ctx:
        def sb(name, shape, dt=F32):
            return ctx.enter_context(nc.sbuf_tensor(name, shape, dt))

        def sem(name):
            return ctx.enter_context(nc.semaphore(name))

        x_all = sb("x_all", [P, TILES, D])
        u_ring = sb("u_ring", [P, R, D])
        v_ring = sb("v_ring", [P, R, D])
        h = sb("h", [P, D])
        hT = sb("hT", [P, KC, P])
        h_dot = sb("h_dot", [P, D])
        kT_fox = sb("kT_fox", [P, FH // 2, SEQ])
        kT_sb = sb("kT_sb", [P, SH // 2, SEQ])
        kT_mla = sb("kT_mla", [MD, MH, SEQ])
        v_fox = sb("v_fox", [P, TILES, FW])
        v_sb = sb("v_sb", [P, TILES, SW])
        v_mla = sb("v_mla", [P, TILES, MW])
        qT_fox = sb("qT_fox", [P, FH // 2, P])
        qT_sb = sb("qT_sb", [P, SH // 2, P])
        qT_mla = sb("qT_mla", [MD, MH, P])
        ffn_gain = sb("ffn_gain", [P, DEPTH, D])
        gT_attn = sb("gT_attn", [P, DEPTH, KC])
        gT_out = sb("gT_out", [P, DEPTH, KC])
        gT_lat = sb("gT_lat", [P, DEPTH, 3])
        gate_b = sb("gate_b", [P, DEPTH, FH])
        w_uq_sb = sb("w_uq_sb", [P, DEPTH, 2, MH * MD])
        w_ukv_sb = sb("w_ukv_sb", [P, DEPTH, MH * 2 * HD])
        keys_sb = sb("keys_sb", [P, DEPTH, 2, NK])
        consts = sb("consts", [P, KW])
        w_ring = sb("w_ring", [P, WSLOTS, KC, WMAX])
        w_kf = sb("w_kf", [P, KC, ROPE + FH])
        mask = sb("mask", [P, SEQ + 1])
        scr = sb("scr", [P, 6, SEQ])
        c_all = sb("c_all", [P, TILES + 1, FH])
        c_cur = sb("c_cur", [P, FH])
        ncT = sb("ncT", [FH, SEQ])
        fl = sb("fl", [P, 4, FH])
        stat = sb("stat", [P, 32])
        rsum = sb("rsum", [P, HEADS])
        rinv = sb("rinv", [P, HEADS])
        nmax = sb("nmax", [P, HEADS])
        top = sb("top", [P, 8, TOPK])
        top_i = sb("top_i", [P, 8, TOPK], U32)
        top_f = sb("top_f", [P, 8, TOPK])
        best = sb("best", [P, PH, TOPK])
        pos = sb("pos", [P, 4, TOPK], U32)
        gsum = sb("gsum", [P, 2, PH])
        ids = sb("ids", [P, 2 * PICKS], U32)
        gates = sb("gates", [P, 2 * PICKS])
        ids_f = sb("ids_f", [P, PICKS])
        layer_off = sb("layer_off", [P, DEPTH])
        stage_u = sb("stage_u", [P, R], U32)
        stage_v = sb("stage_v", [P, R], U32)
        dots = sb("dots", [P, R])
        gel = sb("gel", [P, R])
        coef = sb("coef", [P, R])
        diag = sb("diag", [P, PE, P])
        zero_bf = sb("zero_bf", [32, SEQ], BF16)

        pos_f = qT_fox[:, 0, :].rearrange("p (a n) -> p a n", a=2)
        key_f = qT_fox[:, 1, :].rearrange("p (a n) -> p a n", a=2)
        pos_h = qT_fox[:, 2, :].bitcast(U32).rearrange("p (a n) -> p a n", a=2)
        lat = scr[:, 3, 0:QR + KR]
        latT = scr[:, 5, 0:3 * P].rearrange("p (a n) -> p a n", n=P)
        sc = scr[:, 0:2, :]
        pr = scr[:, 2:4, :]
        pt = scr[:, 4:6, :]
        q_rows = scr[:, 0, 0:(MH + 1) * MD].rearrange("p (h d) -> p h d", d=MD)
        rope_a = scr[:, 1, 0:(MH + 1) * ROPE].rearrange("p (h k d) -> p h k d", h=MH + 1, k=2)
        rope_b = scr[:, 1, 256:256 + (MH + 1) * ROPE].rearrange("p (h k d) -> p h k d", h=MH + 1, k=2)
        k_rows = scr[:, 2, 0:MH * MD].rearrange("p (h d) -> p h d", d=MD)
        key_s = scr[:, 0:2, :].rearrange("p a (b k) -> p (a b) k", k=NK)
        cand = scr[:, 2:4, :].rearrange("p a (b k) -> p (a b) k", k=TOPK * TOPK)
        qT_peer = scr[:, 4:6, :].rearrange("p a (b k) -> p (a b) k", k=P)

        ident = consts[:, K_ID:K_ID + P]
        low_tri = consts[:, K_LT:K_LT + P]
        iota16 = consts[:, K_IOTA:K_IOTA + TOPK]

        acc = ctx.enter_context(nc.psum_tensor("acc", [P, D], F32))
        pa = ctx.enter_context(nc.psum_tensor("pa", [P, 2, SEQ], F32))
        pb = ctx.enter_context(nc.psum_tensor("pb", [P, 2, SEQ], F32))
        yp = ctx.enter_context(nc.psum_tensor("yp", [P, D], F32))

        s_load = sem("s_load")
        s_zero = sem("s_zero")
        s_w = [sem(f"s_w{i}") for i in range(WSLOTS)]
        s_wkf = sem("s_wkf")
        s_w_free = sem("s_w_free")
        s_wkf_free = sem("s_wkf_free")
        pa_full, pb_full, py_full = sem("pa_full"), sem("pb_full"), sem("py_full")
        pa_free = {e: sem(f"pa_free_{e}") for e in "av"}
        pb_free = {e: sem(f"pb_free_{e}") for e in "av"}
        py_free = {e: sem(f"py_free_{e}") for e in "av"}
        s_dve, s_act = sem("s_dve"), sem("s_act")
        s_past = {e: sem(f"s_past_{e}") for e in ("pe", "act", "dve", "pool")}
        s_ss = sem("s_ss")
        s_ln = sem("s_ln")
        s_var = sem("s_var")
        s_h = sem("s_h")
        s_fz = sem("s_fz")
        s_fl = sem("s_fl")
        s_logf = sem("s_logf")
        s_ccur = sem("s_ccur")
        s_ncT = sem("s_ncT")
        s_hT = sem("s_hT")
        s_gT = sem("s_gT")
        s_latT = sem("s_latT")
        s_qr = sem("s_qr")
        s_kr = sem("s_kr")
        s_knope = sem("s_knope")
        s_qk = sem("s_qk")
        s_mask = sem("s_mask")
        s_sc = sem("s_sc")
        s_sp = sem("s_sp")
        s_arg = sem("s_arg")
        s_p = sem("s_p")
        s_pt = sem("s_pt")
        s_pread = sem("s_pread")
        s_pv = sem("s_pv")
        s_y = sem("s_y")
        s_peerq = sem("s_peerq")
        s_keys = sem("s_keys")
        s_keysfree = sem("s_keysfree")
        s_best = sem("s_best")
        s_bexp = sem("s_bexp")
        s_ids = sem("s_ids")
        s_stage_u = sem("s_stage_u")
        s_stage_v = sem("s_stage_v")
        s_u = [sem(f"s_u{i}") for i in range(R)]
        s_v = [sem(f"s_v{i}") for i in range(R)]
        s_dot = sem("s_dot")
        s_mm = sem("s_mm")
        s_axpy = sem("s_axpy")
        s_gel = sem("s_gel")
        s_coef = sem("s_coef")
        s_diag = sem("s_diag")
        s_acc = sem("s_acc")
        s_acc_free = sem("s_acc_free")
        s_fin = sem("s_fin")
        s_out = sem("s_out")

        block = ctx.enter_context(nc.Block())

        def bc(ap2, axis, count):
            return ap2.unsqueeze(axis).to_broadcast(
                [*ap2.shape[:axis], count, *ap2.shape[axis:]])

        LOADS = []

        @block.sync
        def _(sp):
            def load(dst, src):
                sp.dma_start(dst, src).then_inc(s_load, 16)
                LOADS.append(1)

            load(x_all[:], x_d.rearrange("b (t p) d -> p (b t) d", p=P))
            load(consts[:], consts_d)
            load(gT_attn[:], attn_gT)
            load(gT_out[:], out_gT)
            load(gT_lat[:], lat_gT)
            load(w_uq_sb[:], w_uq.rearrange("l (c p) n -> p l c n", p=P))
            load(w_ukv_sb[:], w_ukv.rearrange("l p n -> p l n"))
            load(keys_sb[:], keys_T)
            load(gate_b[:], fgate_b.rearrange("l n -> (l n)").unsqueeze(0).to_broadcast([P, DEPTH * FH])
                 .rearrange("p (l n) -> p l n", l=DEPTH))
            load(ffn_gain[:], ffn_g.rearrange("l n -> (l n)").unsqueeze(0).to_broadcast([P, DEPTH * D])
                 .rearrange("p (l n) -> p l n", l=DEPTH))
            with sp.Fori(0, STEPS) as n:
                layer = n // TILES
                for i, (m, c, w) in enumerate(BLOCKS):
                    sp.wait_ge(s_w_free, n * NB + i + 1)
                    src = {"in": w_in, "out": w_out, "q": w_q}[m]
                    sp.dma_start(w_ring[:, i % WSLOTS, :, 0:w],
                                 src[bass.ds(layer, 1), :, c:c + w].rearrange("l (c p) n -> p (l c) n", p=P)
                                 ).then_inc(s_w[i % WSLOTS], 16)
                    if i == 0:
                        sp.wait_ge(s_wkf_free, n + 1)
                        sp.dma_start(w_kf[:, :, 0:ROPE],
                                     w_in[bass.ds(layer, 1), :, C_KR:C_KR + ROPE]
                                     .rearrange("l (c p) n -> p (l c) n", p=P)).then_inc(s_wkf, 16)
                        sp.dma_start(w_kf[:, :, ROPE:ROPE + FH],
                                     w_in[bass.ds(layer, 1), :, C_FL:C_FL + FH]
                                     .rearrange("l (c p) n -> p (l c) n", p=P)).then_inc(s_wkf, 16)
            sp.wait_ge(s_ids, STEPS)
            sp.dma_start(ffn_gain[:, 0, :], final_g.unsqueeze(0).to_broadcast([P, D])).then_inc(s_load, 16)
            for t in range(TILES):
                sp.wait_ge(s_fin, t + 1)
                sp.dma_start(out_d[0, t * P:(t + 1) * P, :], x_all[:, t, :]).then_inc(s_out, 16)
            sp.wait_ge(s_out, 16 * TILES)

        NLOADS = 16 * len(LOADS)

        @block.gpsimd
        def _(pool):
            for b in (kT_fox, kT_sb, kT_mla, v_fox, v_sb, v_mla, c_all, ncT, zero_bf):
                nc.gpsimd.memset(b[:], 0.0).then_inc(s_zero, 1)
            for l in range(DEPTH):
                nc.gpsimd.memset(layer_off[:, l:l + 1], float(l * EXPERTS)).then_inc(s_zero, 1)
            def rows_of_u(m, it, q):
                pool.wait_ge(s_dot, m * PICKS + it * R + (q + 1) * G)
                pool.sem_inc(s_past["pool"], 1)
                nc.gpsimd.tensor_copy(stage_u[:, q * G:q * G + G],
                                      ids[:, bass.ds((m % 2) * PICKS + it * R + q * G, G)]).then_inc(s_stage_u, 1)
                pool.wait_ge(s_stage_u, m * GROUPS + it * 2 + q + 1)
                pool.sem_inc(s_past["pool"], 1)
                for j in range(q * G, q * G + G):
                    pool.indirect_dma_start(
                        out=u_ring[:, j, :], out_offset=None, in_=u_d,
                        in_offset=bass.IndirectOffsetOnAxis(ap=stage_u[:, j:j + 1], axis=0)).then_inc(s_u[j], 16)

            def rows_of_v(m, it, q):
                pool.wait_ge(s_mm, (m * GROUPS + it * 2 + q + 1) * PE)
                pool.wait_ge(s_axpy, (m * GROUPS + it * 2 + q + 1) * VE)
                pool.sem_inc(s_past["pool"], 1)
                nc.gpsimd.tensor_copy(stage_v[:, q * G:q * G + G],
                                      ids[:, bass.ds((m % 2) * PICKS + it * R + q * G, G)]).then_inc(s_stage_v, 1)
                pool.wait_ge(s_stage_v, m * GROUPS + it * 2 + q + 1)
                pool.sem_inc(s_past["pool"], 1)
                for j in range(q * G, q * G + G):
                    pool.indirect_dma_start(
                        out=v_ring[:, j, :], out_offset=None, in_=v_d,
                        in_offset=bass.IndirectOffsetOnAxis(ap=stage_v[:, j:j + 1], axis=0)).then_inc(s_v[j], 16)

            with pool.Fori(0, STEPS) as m:
                pool.wait_ge(s_ids, m + 1)
                pool.sem_inc(s_past["pool"], 1)
                for q in range(2):
                    rows_of_u(m, 0, q)
                with pool.Fori(0, ITS - 1) as it:
                    for q in range(2):
                        rows_of_v(m, it, q)
                        rows_of_u(m, it + 1, q)
                for q in range(2):
                    rows_of_v(m, ITS - 1, q)

        @block.tensor
        def _(pe):
            def fill(n, ring, name, sems, label):
                b = ring.before(n, label)
                if b is not None:
                    pe.wait_ge(sems[b[0]], b[1])

            def past():
                pe.sem_inc(s_past["pe"], 1)

            def transposes(n, label, srcs, rows=P):
                fill(n, PB, "pb", pb_free, label)
                past()
                for i, s in enumerate(srcs):
                    mm = nc.tensor.transpose(pb[0:rows, PB.slot(label), i * P:(i + 1) * P], s, ident)
                return mm

            def weights(n, i):
                pe.wait_ge(s_w[i % WSLOTS], (n * (NB // WSLOTS) + i // WSLOTS + 1) * 16)

            def cols_T(n, i, label):
                w = BLOCKS[i][2]
                weights(n, i)
                fill(n, PA, "pa", pa_free, label)
                past()
                for j in range(w // P):
                    for c in range(KC):
                        mm = nc.tensor.matmul(pa[:, PA.slot(label), j * P:(j + 1) * P],
                                              w_ring[:, i % WSLOTS, c, j * P:(j + 1) * P], hT[:, c, :],
                                              start=(c == 0), stop=(c == KC - 1))
                mm.then_inc(pa_full, 1)
                pe.wait_ge(pa_full, PA.full(n, label))
                pe.sem_inc(s_w_free, 1)

            def rows_of(n, i, label):
                w = BLOCKS[i][2]
                weights(n, i)
                fill(n, PA, "pa", pa_free, label)
                past()
                for c in range(KC):
                    mm = nc.tensor.matmul(pa[:, PA.slot(label), 0:w], hT[:, c, :], w_ring[:, i % WSLOTS, c, 0:w],
                                          start=(c == 0), stop=(c == KC - 1))
                mm.then_inc(pa_full, 1)
                pe.wait_ge(pa_full, PA.full(n, label))
                pe.sem_inc(s_w_free, 1)

            def mixer(n):
                tile, layer = n % TILES, n // TILES
                pe.wait_ge(s_h, 4 * n + 1)
                for j in range(2):
                    transposes(n, f"hT{j}", [h[:, (4 * j + i) * P:(4 * j + i + 1) * P] for i in range(4)]
                               ).then_inc(pb_full, 1)
                rows(n, "norm")
                pe.wait_ge(s_hT, 4 * n + 2)
                cols_T(n, 0, "fq")
                rows(n, "fq")
                cols_T(n, 1, "fk")
                rows(n, "fk")
                rows_of(n, 2, "fv")
                rows(n, "fv")
                rows_of(n, 3, "cc")
                pe.wait_ge(s_wkf, 32 * (n + 1))
                fill(n, PA, "pa", pa_free, "kf")
                past()
                for c in range(KC):
                    mm = nc.tensor.matmul(pa[:, PA.slot("kf"), 0:ROPE + FH], hT[:, c, :], w_kf[:, c, :],
                                          start=(c == 0), stop=(c == KC - 1))
                mm.then_inc(pa_full, 1)
                pe.wait_ge(pa_full, PA.full(n, "kf"))
                pe.sem_inc(s_wkf_free, 1)
                rows(n, "cc")
                cols_T(n, 4, "sq")
                rows(n, "sq")
                cols_T(n, 5, "sk")
                rows(n, "sk")
                rows_of(n, 6, "sv")
                rows(n, "sv")
                pe.wait_ge(s_logf, n + 1)
                fill(n, PA, "pa", pa_free, "cum")
                past()
                nc.tensor.matmul(pa[:, PA.slot("cum"), 0:FH], low_tri, fl[:, 3, :], start=True, stop=False)
                nc.tensor.matmul(pa[:, PA.slot("cum"), 0:FH], ident[:, P - 1:P].to_broadcast([P, P]),
                                 c_all[:, bass.ds(tile, 1), :].rearrange("p a n -> p (a n)"),
                                 start=False, stop=True).then_inc(pa_full, 1)
                pe.wait_ge(s_ccur, n + 1)
                transposes(n, "ncT", [c_cur[:]], rows=FH).then_inc(pb_full, 1)
                pe.wait_ge(s_h, 4 * n + 2)
                transposes(n, "cqT", [lat[:, i * P:(i + 1) * P] for i in range(3)]).then_inc(pb_full, 1)
                rows(n, "lat")
                pe.wait_ge(s_latT, n + 1)
                fill(n, PA, "pa", pa_free, "qup")
                past()
                for c in range(2):
                    mm = nc.tensor.matmul(pa[:, PA.slot("qup"), 0:MH * MD], latT[:, c, :],
                                          w_uq_sb[:, bass.ds(layer, 1), c, :].rearrange("p a n -> p (a n)"),
                                          start=(c == 0), stop=(c == 1))
                mm.then_inc(pa_full, 1)
                fill(n, PA, "pa", pa_free, "kvup")
                past()
                nc.tensor.matmul(pa[:, PA.slot("kvup"), :], latT[:, 2, :],
                                 w_ukv_sb[:, bass.ds(layer, 1), :].rearrange("p a n -> p (a n)"),
                                 start=True, stop=True).then_inc(pa_full, 1)
                rows(n, "kvup")
                pe.wait_ge(s_qr, n + 1)
                transposes(n, "qTm", [q_rows[:, i, :] for i in range(MH)], rows=MD).then_inc(pb_full, 1)
                pe.wait_ge(s_kr, n + 1)
                pe.wait_ge(s_knope, n + 1)
                transposes(n, "kTm", [k_rows[:, i, :] for i in range(MH)], rows=MD).then_inc(pb_full, 1)
                pe.wait_ge(s_ncT, n + 1)
                pe.wait_ge(s_qk, n + 1)

            def scores(n, i):
                lab = f"s{i}"
                fill(n, PA, "pa", pa_free, lab)
                past()
                o = pa[:, PA.slot(lab), :]
                if i < FH:
                    r = slice(64 * (i % 2), 64 * (i % 2) + 64)
                    nc.tensor.matmul(o, qT_fox[r, i // 2, :], kT_fox[r, i // 2, :], start=True, stop=False)
                    mm = nc.tensor.matmul(o, ident[0:FH, i:i + 1].to_broadcast([FH, P]), ncT[:, :],
                                          start=False, stop=True)
                elif i < FH + MH:
                    mm = nc.tensor.matmul(o, qT_mla[:, i - FH, :], kT_mla[:, i - FH, :], start=True, stop=True)
                else:
                    k = i - FH - MH
                    r = slice(64 * (k % 2), 64 * (k % 2) + 64)
                    mm = nc.tensor.matmul(o, qT_sb[r, k // 2, :], kT_sb[r, k // 2, :], start=True, stop=True)
                mm.then_inc(pa_full, 1)

            def turn(n, i):
                pe.wait_ge(s_p, n * HEADS + i + 1)
                transposes(n, f"p{i}", [pr[:, i % 2, b * P:(b + 1) * P] for b in range(TILES)]
                           ).then_inc(pb_full, 1)

            def pv(n, i):
                pe.wait_ge(s_pt, n * HEADS + i + 1)
                past()
                for b in range(TILES):
                    if i < FH:
                        v = v_fox[:, b, i * HD:(i + 1) * HD]
                    elif i < FH + MH:
                        v = v_mla[:, b, (i - FH) * HD:(i - FH + 1) * HD]
                    else:
                        v = v_sb[:, b, (i - FH - MH) * HD:(i - FH - MH + 1) * HD]
                    mm = nc.tensor.matmul(yp[:, i * HD:(i + 1) * HD], pt[:, i % 2, b * P:(b + 1) * P], v,
                                          start=(b == 0), stop=(b == TILES - 1))
                mm.then_inc(s_pv, 1)
                if i == HEADS - 1:
                    pe.wait_ge(s_pv, (n + 1) * HEADS)
                    pe.sem_inc(py_full, 1)

            def attention(n):
                for i in range(HEADS + 2):
                    if i < HEADS:
                        scores(n, i)
                    if 1 <= i <= HEADS:
                        turn(n, i - 1)
                    if i >= 2:
                        pv(n, i - 2)
                    if i % 2 and i < HEADS:
                        rows(n, f"head{i}")

            def output(n):
                rows(n, "y")
                pe.wait_ge(s_h, 4 * n + 3)
                for j in range(2):
                    transposes(n, f"yT{j}", [h[:, (4 * j + i) * P:(4 * j + i + 1) * P] for i in range(4)]
                               ).then_inc(pb_full, 1)
                pe.wait_ge(s_hT, 4 * n + 4)
                for j in range(3):
                    rows_of(n, 7 + j, f"wo{j}")
                    if j == 0:
                        rows(n, "wo")

            def routing(n):
                layer = n // TILES
                rows(n, "ffn")
                pe.wait_ge(s_h, 4 * n + 4)
                for j in range(2):
                    transposes(n, f"gT{j}", [h[:, (4 * j + i) * P:(4 * j + i + 1) * P] for i in range(4)]
                               ).then_inc(pb_full, 1)
                pe.wait_ge(s_gT, 2 * n + 2)
                for g in range(2):
                    for j in range(3):
                        cols_T(n, 10 + 3 * g + j, f"wq{3 * g + j}")
                        rows(n, f"g{g}{'abc'[j]}")
                    pe.wait_ge(s_peerq, 6 * n + 3 * g + 3)
                    fill(n, PY, "py", py_free, f"ks{g}")
                    past()
                    for k in range(8):
                        mm = nc.tensor.matmul(yp[:, k * NK:(k + 1) * NK], qT_peer[:, k, :],
                                              keys_sb[:, bass.ds(layer, 1), k % 2, :].rearrange("p a n -> p (a n)"),
                                              start=True, stop=True)
                    mm.then_inc(py_full, 1)
                    rows(n, f"g{g}d")
                    rows(n, f"g{g}e")
                for ring, sems in ((PA, pa_free), (PB, pb_free), (PY, py_free)):
                    for e in "av":
                        pe.wait_ge(sems[e], (n + 1) * ring.per[e])

            def sum_start(m):
                pe.wait_ge(s_acc_free, m + 1)
                past()
                for c in range(2):
                    nc.tensor.matmul(acc[:, c * 512:c * 512 + 512], zero_bf[:, 0:P], zero_bf[:, :],
                                     start=True, stop=False)

            def sum_rows(m, it, q):
                for i in range(PE):
                    j = q * G + i
                    pe.wait_ge(s_diag, (m * GROUPS + it * 2 + q) * PE + i + 1)
                    pe.wait_ge(s_v[j], (m * ITS + it + 1) * 16)
                    for c in range(2):
                        mm = nc.tensor.matmul(acc[:, c * 512:c * 512 + 512], diag[:, i, :],
                                              v_ring[:, j, c * 512:c * 512 + 512], start=False, stop=False)
                    mm.then_inc(s_mm, 1)

            def sum_end():
                for c in range(2):
                    mm = nc.tensor.matmul(acc[:, c * 512:c * 512 + 512], zero_bf[:, 0:P], zero_bf[:, :],
                                          start=False, stop=True)
                mm.then_inc(s_acc, 1)

            places = Places()

            def rows(n, label):
                if FIRST(n):
                    return
                p = places.next(label)
                if p == 1:
                    sum_start(n - 1)
                if p >= 1:
                    sum_rows(n - 1, *divmod(p - 1, 2))

            def last_rows(n):
                if not FIRST(n):
                    sum_rows(n - 1, *divmod(GROUPS - 1, 2))
                    sum_end()

            pe.wait_ge(s_load, NLOADS)
            pe.wait_ge(s_zero, 9 + DEPTH)
            pe.sem_inc(s_w_free, WSLOTS)
            pe.sem_inc(s_wkf_free, 1)
            pe.sem_inc(s_mm, 2 * PE)

            def step(n):
                mixer(n)
                attention(n)
                output(n)
                routing(n)
                rows(n, "end")
                last_rows(n)

            step(0)
            with pe.Fori(1, STEPS) as n:
                step(n)
            sum_start(STEPS - 1)
            with pe.Fori(0, ITS) as it:
                for q in range(2):
                    sum_rows(STEPS - 1, it, q)
            sum_end()

        @block.scalar
        def _(act):
            links = [0]

            def link(n, ins):
                links[0] += 1
                ins.then_inc(s_act, 1)
                act.wait_ge(s_act, n * ACT_LINKS + links[0])

            def past():
                act.sem_inc(s_past["act"], 1)

            def take(n, ring, full, label):
                act.wait_ge(full, ring.full(n, label))
                past()

            def squares(src, dst, junk):
                return nc.scalar.activation(junk, src, ACT.Square, accum_out=dst)

            def rsqrt(n, k, cols, dst):
                act.wait_ge(s_var, 4 * n + k)
                link(n, nc.scalar.activation(dst, cols, ACT.Ln))
                nc.scalar.activation(dst, dst, ACT.Exp, scale=-0.5).then_inc(s_ln, 1)

            def mixer(n):
                tile, layer = n % TILES, n // TILES
                if not FIRST(n):
                    act.wait_ge(s_acc_free, n)
                    past()
                squares(x_all[:, bass.ds(tile, 1), :].rearrange("p a n -> p (a n)"), stat[:, 0:1],
                        scr[:, 4:6, :].rearrange("p a n -> p (a n)")).then_inc(s_ss, 1)
                rsqrt(n, 1, stat[:, 4:5], stat[:, 8:9])
                past()
                nc.scalar.copy(mask[:], consts[:, bass.ds(K_MASK + (TILES - 1 - tile) * P, SEQ + 1)]).then_inc(s_mask, 1)
                rows(n, "norm")
                take(n, PA, pa_full, "fq")
                nc.scalar.activation(qT_fox[:].rearrange("p a n -> p (a n)"), pa[:, PA.slot("fq"), 0:FW], ACT.Copy,
                                     scale=HD ** -0.5).then_inc(pa_free["a"], 1)
                rows(n, "fq")
                take(n, PA, pa_full, "fk")
                nc.scalar.copy(kT_fox[:, :, bass.ds(tile * P, P)],
                               pa[:, PA.slot("fk"), 0:FW].rearrange("p (a n) -> p a n", n=P)).then_inc(pa_free["a"], 1)
                rows(n, "fk")
                take(n, PA, pa_full, "fv")
                nc.scalar.copy(v_fox[:, bass.ds(tile, 1), :].rearrange("p a n -> p (a n)"),
                               pa[:, PA.slot("fv"), 0:FW]).then_inc(pa_free["a"], 1)
                rows(n, "fv")
                rows(n, "cc")
                act.wait_ge(s_fz, n + 1)
                link(n, nc.scalar.activation(fl[:, 1, :], fl[:, 0, :], ACT.Abs))
                link(n, nc.scalar.activation(fl[:, 1, :], fl[:, 1, :], ACT.Exp, scale=-1.0))
                nc.scalar.activation(fl[:, 1, :], fl[:, 1, :], ACT.Ln, bias=1.0).then_inc(s_fl, 1)
                link(n, squares(lat[:, 0:QR], stat[:, 1:2], scr[:, 4, 0:QR]))
                squares(lat[:, QR:QR + KR], stat[:, 2:3], scr[:, 4, 256:256 + KR]).then_inc(s_ss, 1)
                rsqrt(n, 2, stat[:, 5:7], stat[:, 9:11])
                take(n, PA, pa_full, "sq")
                nc.scalar.activation(qT_sb[:].rearrange("p a n -> p (a n)"), pa[:, PA.slot("sq"), 0:SW], ACT.Copy,
                                     scale=HD ** -0.5).then_inc(pa_free["a"], 1)
                rows(n, "sq")
                take(n, PA, pa_full, "sk")
                nc.scalar.copy(kT_sb[:, :, bass.ds(tile * P, P)],
                               pa[:, PA.slot("sk"), 0:SW].rearrange("p (a n) -> p a n", n=P)).then_inc(pa_free["a"], 1)
                rows(n, "sk")
                take(n, PA, pa_full, "sv")
                nc.scalar.copy(v_sb[:, bass.ds(tile, 1), :].rearrange("p a n -> p (a n)"),
                               pa[:, PA.slot("sv"), 0:SW]).then_inc(pa_free["a"], 1)
                rows(n, "sv")
                rows(n, "lat")
                take(n, PA, pa_full, "kvup")
                kv = pa[:, PA.slot("kvup"), :].rearrange("p (h d) -> p h d", d=2 * HD)
                nc.scalar.copy(k_rows[:, :, 0:NOPE], kv[:, :, 0:NOPE]).then_inc(s_knope, 1)
                nc.scalar.copy(v_mla[:, bass.ds(tile, 1), :].rearrange("p a (h d) -> p (a h) d", d=HD),
                               kv[:, :, NOPE:2 * HD]).then_inc(pa_free["a"], 1)
                rows(n, "kvup")
                take(n, PB, pb_full, "qTm")
                nc.scalar.activation(qT_mla[:].rearrange("p a n -> p (a n)"), pb[0:MD, PB.slot("qTm"), :], ACT.Copy,
                                     scale=MD ** -0.5).then_inc(pb_free["a"], 1)
                take(n, PB, pb_full, "kTm")
                nc.scalar.copy(kT_mla[:, :, bass.ds(tile * P, P)],
                               pb[0:MD, PB.slot("kTm"), :].rearrange("p (a n) -> p a n", n=P)
                               ).then_inc(pb_free["a"], 1)
                act.wait_ge(pa_free["a"], n * PA.per["a"] + 7)
                act.wait_ge(pb_free["a"], n * PB.per["a"] + 2)
                act.sem_inc(s_qk, 1)

            def first(n, i):
                act.wait_ge(s_sc, n * HEADS + i + 1)
                past()
                if i >= 2:
                    act.wait_ge(s_pread, n * HEADS + i - 1)
                    past()
                s, p = sc[:, i % 2, :], pr[:, i % 2, :]
                if i < FH + MH:
                    nc.scalar.activation(p, s, ACT.Exp, scale=-1.0, bias=nmax[:, i:i + 1],
                                         accum_out=rsum[:, i:i + 1]).then_inc(s_p, 1)
                else:
                    link(n, nc.scalar.activation(p, s, ACT.Abs))
                    link(n, nc.scalar.activation(p, p, ACT.Exp, scale=-1.0))
                    nc.scalar.activation(p, p, ACT.Ln, bias=1.0).then_inc(s_sp, 1)

            def second(n, i):
                if i >= FH + MH:
                    act.wait_ge(s_arg, n * SH + i - FH - MH + 1)
                    nc.scalar.activation(pr[:, i % 2, :], pr[:, i % 2, :], ACT.Exp).then_inc(s_p, 1)

            def turned(n, i):
                take(n, PB, pb_full, f"p{i}")
                if i >= 2:
                    act.wait_ge(s_pv, n * HEADS + i - 1)
                    past()
                nc.scalar.copy(pt[:, i % 2, :], pb[:, PB.slot(f"p{i}"), :]).then_inc(s_pt, 1)
                act.wait_ge(s_pt, n * HEADS + i + 1)
                act.sem_inc(pb_free["a"], 1)
                act.sem_inc(s_pread, 1)

            def attention(n):
                for i in range(HEADS + 1):
                    if i < HEADS:
                        first(n, i)
                    if 1 <= i <= HEADS:
                        second(n, i - 1)
                        turned(n, i - 1)
                    if i % 2 and i < HEADS:
                        rows(n, f"head{i}")

            def output(n):
                act.wait_ge(s_y, n + 1)
                past()
                for k, (a, b) in enumerate(((0, FW), (FW, FW + MW), (FW + MW, D))):
                    link(n, squares(h[:, a:b], stat[:, 12 + k:13 + k], scr[:, 0:2, :].rearrange("p a n -> p (a n)")[:, a:b]))
                act.sem_inc(s_ss, 1)
                rsqrt(n, 3, stat[:, 16:19], stat[:, 20:23])
                rows(n, "y")
                rows(n, "wo")
                act.wait_ge(pa_free["v"], n * PA.per["v"] + PA.per["v"])
                past()
                squares(x_all[:, bass.ds(n % TILES, 1), :].rearrange("p a n -> p (a n)"), stat[:, 0:1],
                        scr[:, 4:6, :].rearrange("p a n -> p (a n)")).then_inc(s_ss, 1)
                rsqrt(n, 4, stat[:, 4:5], stat[:, 8:9])
                rows(n, "ffn")

            def routing(n):
                for j in range(2):
                    take(n, PB, pb_full, f"gT{j}")
                    nc.scalar.copy(hT[:, 4 * j:4 * j + 4, :].rearrange("p a n -> p (a n)"), pb[:, PB.slot(f"gT{j}"), :]
                                   ).then_inc(s_gT, 1)
                    act.wait_ge(s_gT, 2 * n + j + 1)
                    act.sem_inc(pb_free["a"], 1)
                for g in range(2):
                    for j in range(3):
                        i = 3 * g + j
                        w = BLOCKS[10 + i][2]
                        take(n, PA, pa_full, f"wq{i}")
                        if g == 1 and j == 0:
                            act.wait_ge(py_full, PY.full(n, "ks0"))
                            past()
                        nc.scalar.copy(qT_peer[:, 3 * j:3 * j + w // P, :].rearrange("p a n -> p (a n)"),
                                       pa[:, PA.slot(f"wq{i}"), 0:w]).then_inc(s_peerq, 1)
                        act.wait_ge(s_peerq, 6 * n + i + 1)
                        act.sem_inc(pa_free["a"], 1)
                        rows(n, f"g{g}{'abc'[j]}")
                    take(n, PY, py_full, f"ks{g}")
                    if g == 1:
                        act.wait_ge(s_keysfree, 2 * n + 1)
                        past()
                    for j in range(2):
                        ins = nc.scalar.copy(key_s[:, 4 * j:4 * j + 4, :].rearrange("p a n -> p (a n)"),
                                             yp[:, j * 512:j * 512 + 512])
                        link(n, ins)
                    act.sem_inc(s_keys, 1)
                    act.sem_inc(py_free["a"], 1)
                    rows(n, f"g{g}d")
                    rows(n, f"g{g}e")
                act.wait_ge(s_best, n + 1)
                nc.scalar.activation(best[:], best[:], ACT.Exp).then_inc(s_bexp, 1)

            def weigh(m, it, q):
                k = m * GROUPS + it * 2 + q
                act.wait_ge(s_dot, m * PICKS + it * R + (q + 1) * G + R)
                nc.scalar.activation(gel[:, q * G:q * G + G], dots[:, q * G:q * G + G], ACT.Gelu
                                     ).then_inc(s_gel, 1)
                act.wait_ge(s_gel, k + 1 + 2)
                act.wait_ge(s_axpy, (k + 1) * VE)
                past()
                for j in range(q * G, q * G + G):
                    ins = nc.scalar.activation(coef[:, j:j + 1], gel[:, j:j + 1], ACT.Copy,
                                               scale=gates[:, bass.ds((m % 2) * PICKS + it * R + j, 1)])
                ins.then_inc(s_coef, 1)
                act.wait_ge(s_coef, k + 1)
                for i in range(PE):
                    act.wait_ge(s_mm, (k + 1) * PE + i + 1)
                    nc.scalar.activation(diag[:, i, :], ident, ACT.Copy, scale=coef[:, q * G + i:q * G + i + 1]
                                         ).then_inc(s_diag, 1)

            places = Places()

            def rows(n, label):
                if FIRST(n):
                    return
                p = places.next(label)
                if p >= 1:
                    weigh(n - 1, *divmod(p - 1, 2))

            act.wait_ge(s_load, NLOADS)
            act.wait_ge(s_zero, 9 + DEPTH)

            def step(n):
                links[0] = 0
                mixer(n)
                attention(n)
                output(n)
                routing(n)
                rows(n, "end")
                if not FIRST(n):
                    weigh(n - 1, *divmod(GROUPS - 1, 2))
                assert links[0] == ACT_LINKS, links

            step(0)
            with act.Fori(1, STEPS) as n:
                step(n)
            act.wait_ge(s_ids, STEPS)
            act.sem_inc(s_past["act"], 1)
            with act.Fori(0, ITS) as it:
                for q in range(2):
                    weigh(STEPS - 1, it, q)
            act.wait_ge(s_acc_free, STEPS + 1)
            spare = [h[:], h_dot[:]] + [scr[:, k:k + 2, :].rearrange("p a n -> p (a n)") for k in (2, 4)]
            for t in range(TILES):
                squares(x_all[:, t, :], stat[:, 24 + t:25 + t], spare[t]).then_inc(s_ss, 1)
            act.wait_ge(s_var, 4 * STEPS + 1)
            nc.scalar.activation(stat[:, 8:12], stat[:, 4:8], ACT.Ln).then_inc(s_act, 1)
            act.wait_ge(s_act, STEPS * ACT_LINKS + 1)
            nc.scalar.activation(stat[:, 8:12], stat[:, 8:12], ACT.Exp, scale=-0.5).then_inc(s_ln, 1)

        @block.vector
        def _(dve):
            links = [0]

            def link(n, ins):
                links[0] += 1
                ins.then_inc(s_dve, 1)
                dve.wait_ge(s_dve, n * DVE_LINKS + links[0])

            def past():
                dve.sem_inc(s_past["dve"], 1)

            def take(n, ring, full, label):
                dve.wait_ge(full, ring.full(n, label))
                past()

            def refine(n, k, var, est, dst, tmp):
                dve.wait_ge(s_ln, 4 * n + k)
                link(n, nc.vector.tensor_tensor(tmp, est, est, ALU.mult))
                link(n, nc.vector.tensor_tensor(tmp, tmp, var, ALU.mult))
                link(n, nc.vector.tensor_scalar(tmp, tmp, -0.5, 1.5, ALU.mult, ALU.add))
                link(n, nc.vector.tensor_tensor(dst, est, tmp, ALU.mult))

            def variance(dst, src, width):
                return nc.vector.tensor_scalar(dst, src, 1.0 / width, EPS, ALU.mult, ALU.add)

            def x_tile(n):
                return x_all[:, bass.ds(n % TILES, 1), :].rearrange("p a n -> p (a n)")

            def mixer(n):
                tile, layer = n % TILES, n // TILES
                dve.wait_ge(s_ss, 4 * n + 1)
                variance(stat[:, 4:5], stat[:, 0:1], D).then_inc(s_var, 1)
                refine(n, 1, stat[:, 4:5], stat[:, 8:9], stat[:, 30:31], stat[:, 31:32])
                past()
                nc.vector.tensor_scalar(h[:], x_tile(n), stat[:, 30:31], None, ALU.mult).then_inc(s_h, 1)

                def turned(labels, gT):
                    for j, lab in enumerate(labels):
                        take(n, PB, pb_full, lab)
                        nc.vector.tensor_tensor(
                            hT[:, 4 * j:4 * j + 4, :], pb[:, PB.slot(lab), :].rearrange("p (a n) -> p a n", n=P),
                            bc(gT[:, bass.ds(layer, 1), 4 * j:4 * j + 4].rearrange("p a n -> p (a n)"), 2, P),
                            ALU.mult).then_inc(s_hT, 1)
                        dve.wait_ge(s_hT, 4 * n + j + (1 if gT is gT_attn else 3))
                        dve.sem_inc(pb_free["v"], 1)

                rows(n, "norm")
                turned(["hT0", "hT1"], gT_attn)
                rows(n, "fq")
                rows(n, "fk")
                rows(n, "fv")
                take(n, PA, pa_full, "cc")
                nc.vector.tensor_copy(lat, pa[:, PA.slot("cc"), 0:QR + KR]).then_inc(pa_free["v"], 1)
                take(n, PA, pa_full, "kf")
                nc.vector.tensor_copy(q_rows[:, MH, NOPE:MD], pa[:, PA.slot("kf"), 0:ROPE])
                nc.vector.tensor_tensor(fl[:, 0, :], pa[:, PA.slot("kf"), ROPE:ROPE + FH],
                                        gate_b[:, bass.ds(layer, 1), :].rearrange("p a n -> p (a n)"),
                                        ALU.add).then_inc(pa_free["v"], 1)
                dve.wait_ge(pa_free["v"], n * PA.per["v"] + 2)
                dve.sem_inc(s_fz, 1)
                rows(n, "cc")
                dve.wait_ge(s_fl, n + 1)
                nc.vector.scalar_tensor_tensor(out=fl[:, 3, :], in0=fl[:, 0, :], scalar=0.0, in1=fl[:, 1, :],
                                               op0=ALU.min, op1=ALU.subtract).then_inc(s_logf, 1)
                dve.wait_ge(s_ss, 4 * n + 2)
                link(n, variance(stat[:, 5:6], stat[:, 1:2], QR))
                variance(stat[:, 6:7], stat[:, 2:3], KR).then_inc(s_var, 1)
                refine(n, 2, stat[:, 5:7], stat[:, 9:11], stat[:, 26:28], stat[:, 28:30])
                link(n, nc.vector.tensor_scalar(lat[:, 0:QR], lat[:, 0:QR], stat[:, 26:27], None, ALU.mult))
                nc.vector.tensor_scalar(lat[:, QR:], lat[:, QR:], stat[:, 27:28], None, ALU.mult).then_inc(s_h, 1)
                rows(n, "sq")
                rows(n, "sk")
                rows(n, "sv")
                take(n, PA, pa_full, "cum")
                nc.vector.tensor_copy(c_cur[:], pa[:, PA.slot("cum"), 0:FH]).then_inc(s_ccur, 1)
                nc.vector.tensor_copy(c_all[:, bass.ds(tile + 1, 1), :].rearrange("p a n -> p (a n)"),
                                      pa[:, PA.slot("cum"), 0:FH]).then_inc(pa_free["v"], 1)
                take(n, PB, pb_full, "ncT")
                nc.vector.tensor_scalar(ncT[:, bass.ds(tile * P, P)], pb[0:FH, PB.slot("ncT"), 0:P], -1.0, None,
                                        ALU.mult).then_inc(s_ncT, 1)
                dve.wait_ge(s_ncT, n + 1)
                dve.sem_inc(pb_free["v"], 1)
                take(n, PB, pb_full, "cqT")
                nc.vector.tensor_tensor(
                    latT, pb[:, PB.slot("cqT"), 0:3 * P].rearrange("p (a n) -> p a n", n=P),
                    bc(gT_lat[:, bass.ds(layer, 1), :].rearrange("p a n -> p (a n)"), 2, P),
                    ALU.mult).then_inc(s_latT, 1)
                dve.wait_ge(s_latT, n + 1)
                dve.sem_inc(pb_free["v"], 1)
                rows(n, "lat")
                take(n, PA, pa_full, "qup")
                nc.vector.tensor_copy(q_rows[:, 0:MH, :],
                                      pa[:, PA.slot("qup"), 0:MH * MD].rearrange("p (h d) -> p h d", d=MD)
                                      ).then_inc(pa_free["v"], 1)
                dve.wait_ge(pa_free["v"], n * PA.per["v"] + 4)
                hf = ROPE // 2
                rot = q_rows[:, :, NOPE:MD].rearrange("p h (k d) -> p h k d", k=2)
                past()
                for k in range(2):
                    t = consts[:, bass.ds(tile * ROPE + K_ROPE, hf)]
                    link(n, nc.vector.tensor_tensor(rope_a[:, :, k, :], rot[:, :, k, :], bc(t, 1, MH + 1), ALU.mult))
                    t = consts[:, bass.ds(tile * ROPE + K_ROPE + hf, hf)]
                    link(n, nc.vector.tensor_tensor(rope_b[:, :, k, :], rot[:, :, k, :], bc(t, 1, MH + 1), ALU.mult))
                link(n, nc.vector.tensor_tensor(rot[:, :, 0, :], rope_a[:, :, 0, :], rope_b[:, :, 1, :], ALU.subtract))
                link(n, nc.vector.tensor_tensor(rot[:, :, 1, :], rope_b[:, :, 0, :], rope_a[:, :, 1, :], ALU.add))
                dve.sem_inc(s_qr, 1)
                nc.vector.tensor_copy(k_rows[:, :, NOPE:MD],
                                      q_rows[:, MH:MH + 1, NOPE:MD].to_broadcast([P, MH, ROPE])).then_inc(s_kr, 1)
                rows(n, "kvup")
                dve.wait_ge(s_mask, n + 1)
                dve.wait_ge(s_qk, n + 1)
                past()

            def first(n, i):
                take(n, PA, pa_full, f"s{i}")
                if 2 <= i:
                    dve.wait_ge(s_p, n * HEADS + i - 1)
                    past()
                s, z = sc[:, i % 2, :], pa[:, PA.slot(f"s{i}"), :]
                if i < FH + MH:
                    nc.vector.tensor_tensor_reduce(s, z, mask[:, 0:SEQ], -1.0, -NEG, ALU.add, ALU.min,
                                                   nmax[:, i:i + 1]).then_inc(s_sc, 1)
                else:
                    nc.vector.tensor_tensor(s, z, mask[:, 1:SEQ + 1], ALU.add).then_inc(s_sc, 1)
                dve.wait_ge(s_sc, n * HEADS + i + 1)
                dve.sem_inc(pa_free["v"], 1)

            def second(n, i):
                k = i - FH - MH
                if k < 0:
                    return
                s, p = sc[:, i % 2, :], pr[:, i % 2, :]
                dve.wait_ge(s_sp, n * SH + k + 1)
                link(n, nc.vector.scalar_tensor_tensor(out=p, in0=s, scalar=0.0, in1=p, op0=ALU.max, op1=ALU.add))
                back = pr[:, i % 2, ::-1]
                link(n, nc.vector.tensor_tensor_scan(back, consts[:, K_LT + P - 1:K_LT + P].to_broadcast([P, SEQ]),
                                                     back, 0.0, ALU.mult, ALU.add))
                nc.vector.tensor_tensor(p, s, p, ALU.subtract).then_inc(s_arg, 1)

            def attention(n):
                for i in range(HEADS + 1):
                    if i < HEADS:
                        first(n, i)
                    if i >= 1:
                        second(n, i - 1)
                    if i % 2 and i < HEADS:
                        rows(n, f"head{i}")

            def output(n):
                layer = n // TILES
                dve.wait_ge(s_p, (n + 1) * HEADS)
                link(n, nc.vector.reciprocal(rinv[:, 0:FH + MH], rsum[:, 0:FH + MH]))
                take(n, PY, py_full, "y")
                link(n, nc.vector.tensor_tensor(
                    h[:, 0:FW + MW].rearrange("p (h d) -> p h d", d=HD),
                    yp[:, 0:FW + MW].rearrange("p (h d) -> p h d", d=HD),
                    bc(rinv[:, 0:FH + MH], 2, HD), ALU.mult))
                link(n, nc.vector.tensor_copy(h[:, FW + MW:D], yp[:, FW + MW:D]))
                dve.sem_inc(s_y, 1)
                dve.sem_inc(py_free["v"], 1)
                dve.wait_ge(s_ss, 4 * n + 3)
                link(n, variance(stat[:, 16:17], stat[:, 12:13], FW))
                link(n, variance(stat[:, 17:18], stat[:, 13:14], MW))
                variance(stat[:, 18:19], stat[:, 14:15], SW).then_inc(s_var, 1)
                refine(n, 3, stat[:, 16:19], stat[:, 20:23], stat[:, 23:26], stat[:, 26:29])
                for k, (a, b) in enumerate(((0, FW), (FW, FW + MW), (FW + MW, D))):
                    ins = nc.vector.tensor_scalar(h[:, a:b], h[:, a:b], stat[:, 23 + k:24 + k], None, ALU.mult)
                    if k == 2:
                        ins.then_inc(s_h, 1)
                    else:
                        link(n, ins)
                rows(n, "y")
                for j in range(2):
                    lab = f"yT{j}"
                    take(n, PB, pb_full, lab)
                    nc.vector.tensor_tensor(
                        hT[:, 4 * j:4 * j + 4, :], pb[:, PB.slot(lab), :].rearrange("p (a n) -> p a n", n=P),
                        bc(gT_out[:, bass.ds(layer, 1), 4 * j:4 * j + 4].rearrange("p a n -> p (a n)"), 2, P),
                        ALU.mult).then_inc(s_hT, 1)
                    dve.wait_ge(s_hT, 4 * n + j + 3)
                    dve.sem_inc(pb_free["v"], 1)
                for j in range(3):
                    i = 7 + j
                    c, w = BLOCKS[i][1], BLOCKS[i][2]
                    take(n, PA, pa_full, f"wo{j}")
                    xs = x_all[:, bass.ds(n % TILES, 1), c:c + w].rearrange("p a n -> p (a n)")
                    nc.vector.tensor_tensor(xs, xs, pa[:, PA.slot(f"wo{j}"), 0:w], ALU.add).then_inc(pa_free["v"], 1)
                rows(n, "wo")
                dve.wait_ge(s_ss, 4 * n + 4)
                variance(stat[:, 4:5], stat[:, 0:1], D).then_inc(s_var, 1)
                refine(n, 4, stat[:, 4:5], stat[:, 8:9], stat[:, 30:31], stat[:, 31:32])
                past()
                nc.vector.scalar_tensor_tensor(
                    out=h[:], in0=x_tile(n), scalar=stat[:, 30:31],
                    in1=ffn_gain[:, bass.ds(layer, 1), :].rearrange("p a n -> p (a n)"),
                    op0=ALU.mult, op1=ALU.mult).then_inc(s_h, 1)
                rows(n, "ffn")

            def best16(n, src, vals, idx):
                past()
                for a, b in ((0, 8), (8, 16)):
                    for s, v in zip(src, vals):
                        ins = nc.vector.max(v[:, a:b], s)
                    link(n, ins)
                    past()
                    for s, v, i in zip(src, vals, idx):
                        ins = nc.vector.max_index(i[:, a:b], v[:, a:b], s)
                    link(n, ins)
                    past()
                    if a == 0:
                        for s, v in zip(src, vals):
                            ins = nc.vector.match_replace(out=s, in_to_replace=v[:, a:b], in_values=s, imm_value=GONE)
                        link(n, ins)
                        past()

            def routing(n):
                layer = n // TILES
                for g in range(2):
                    for place in "abc":
                        rows(n, f"g{g}{place}")
                    dve.wait_ge(s_keys, 2 * n + g + 1)
                    best16(n, [key_s[:, k, :] for k in range(8)], [top[:, k, :] for k in range(8)],
                           [top_i[:, k, :] for k in range(8)])
                    link(n, nc.vector.tensor_copy(top_f[:], top_i[:]))
                    rows(n, f"g{g}d")
                    pair = top[:].rearrange("p (h k) n -> p h k n", k=2)
                    for j in range(4):
                        ins = nc.vector.tensor_tensor(cand[:, j, :].rearrange("p (a b) -> p a b", b=TOPK),
                                                bc(pair[:, j, 0, :], 2, TOPK), bc(pair[:, j, 1, :], 1, TOPK), ALU.add)
                    link(n, ins)
                    bs = best[:, 4 * g:4 * g + 4, :]
                    best16(n, [cand[:, j, :] for j in range(4)], [bs[:, j, :] for j in range(4)],
                           [pos[:, j, :] for j in range(4)])
                    flat = pos[:].rearrange("p a n -> p (a n)")
                    nc.vector.tensor_scalar(pos_h[:, 0, :], flat, 4, None, ALU.logical_shift_right)
                    link(n, nc.vector.tensor_scalar(pos_h[:, 1, :], flat, TOPK - 1, None, ALU.bitwise_and))
                    link(n, nc.vector.tensor_copy(pos_f, pos_h))
                    rows(n, f"g{g}e")
                    for k in range(2):
                        hot = cand[:].rearrange("p a n -> p (a n)").rearrange("p (m i) -> p m i", i=TOPK)
                        link(n, nc.vector.tensor_tensor(hot, bc(pos_f[:, k, :], 2, TOPK),
                                                        bc(iota16, 1, 4 * TOPK), ALU.is_equal))
                        for j in range(4):
                            hj = cand[:, j, :].rearrange("p (m i) -> p m i", i=TOPK)
                            ins = nc.vector.tensor_tensor(hj, hj, bc(top_f[:, 2 * j + k, :], 1, TOPK), ALU.mult)
                        link(n, ins)
                        link(n, nc.vector.tensor_reduce(key_f[:, k, :], hot, AX.X, ALU.add))
                    dve.sem_inc(s_keysfree, 1)
                    link(n, nc.vector.scalar_tensor_tensor(out=ids_f[:, 64 * g:64 * g + 64], in0=key_f[:, 0, :],
                                                           scalar=float(NK), in1=key_f[:, 1, :],
                                                           op0=ALU.mult, op1=ALU.add))
                link(n, nc.vector.tensor_copy(gsum[:, 0, :], best[:, :, 0]))
                nc.vector.tensor_tensor(best[:], best[:], bc(gsum[:, 0, :], 2, TOPK), ALU.subtract).then_inc(s_best, 1)
                dve.wait_ge(s_bexp, n + 1)
                link(n, nc.vector.tensor_reduce(gsum[:, 0, :], best[:], AX.X, ALU.add))
                link(n, nc.vector.reciprocal(gsum[:, 1, :], gsum[:, 0, :]))

            def hand_over(n):
                layer = n // TILES
                half = bass.ds((n % 2) * PICKS, PICKS)
                dve.wait_ge(s_dot, n * PICKS + R)
                past()
                nc.vector.tensor_scalar(ids[:, half], ids_f[:], layer_off[:, bass.ds(layer, 1)], None, ALU.add)
                nc.vector.tensor_copy(h_dot[:], h[:])
                link(n, nc.vector.tensor_tensor(gates[:, half].rearrange("p (h n) -> p h n", n=TOPK), best[:],
                                                bc(gsum[:, 1, :], 2, TOPK), ALU.mult))
                dve.sem_inc(s_ids, 1)

            def dot_rows(m, it, q):
                for j in range(q * G, q * G + G):
                    if j % G == 0:
                        dve.wait_ge(s_gel, m * GROUPS + it * 2 + q + 1)
                    dve.wait_ge(s_u[j], (m * ITS + it + 1) * 16)
                    nc.vector.tensor_tensor_reduce(u_ring[:, j, :], u_ring[:, j, :], h_dot[:], 1.0, 0.0,
                                                   ALU.mult, ALU.add, dots[:, j:j + 1]).then_inc(s_dot, 1)

            def add_rows(m, it, q):
                k = m * GROUPS + it * 2 + q
                dve.wait_ge(s_coef, k + 1)
                for i in range(VE):
                    j = q * G + PE + i
                    dve.wait_ge(s_v[j], (m * ITS + it + 1) * 16)
                    dve.wait_ge(s_axpy, k * VE + i + 2 * VE)
                    past()
                    nc.vector.scalar_tensor_tensor(out=x_tile(m), in0=v_ring[:, j, :], scalar=coef[:, j:j + 1],
                                                   in1=x_tile(m), op0=ALU.mult, op1=ALU.add).then_inc(s_axpy, 1)

            def add_experts(m):
                dve.wait_ge(s_acc, m + 1)
                dve.wait_ge(s_axpy, (m + 1) * GROUPS * VE + 2 * VE)
                past()
                nc.vector.tensor_tensor(x_tile(m), x_tile(m), acc[:], ALU.add).then_inc(s_acc_free, 1)

            places = Places()

            def rows(n, label):
                if FIRST(n):
                    return
                p = places.next(label)
                dot_rows(n - 1, *divmod(p, 2))
                if p >= 1:
                    add_rows(n - 1, *divmod(p - 1, 2))

            dve.wait_ge(s_load, NLOADS)
            dve.wait_ge(s_zero, 9 + DEPTH)
            dve.sem_inc(s_dot, R)
            dve.sem_inc(s_gel, 2)
            dve.sem_inc(s_axpy, 2 * VE)
            dve.sem_inc(s_acc_free, 1)

            def step(n):
                links[0] = 0
                mixer(n)
                attention(n)
                output(n)
                routing(n)
                rows(n, "end")
                hand_over(n)
                if not FIRST(n):
                    add_rows(n - 1, *divmod(GROUPS - 1, 2))
                    add_experts(n - 1)
                assert links[0] == DVE_LINKS, links

            step(0)
            with dve.Fori(1, STEPS) as n:
                step(n)
            m = STEPS - 1
            dot_rows(m, 0, 0)
            dot_rows(m, 0, 1)
            add_rows(m, 0, 0)
            with dve.Fori(1, ITS) as it:
                dot_rows(m, it, 0)
                add_rows(m, it - 1, 1)
                dot_rows(m, it, 1)
                add_rows(m, it, 0)
            add_rows(m, ITS - 1, 1)
            add_experts(m)
            base = STEPS * DVE_LINKS
            dve.wait_ge(s_ss, 4 * STEPS + TILES)
            variance(stat[:, 4:8], stat[:, 24:28], D).then_inc(s_var, 1)
            dve.wait_ge(s_ln, 4 * STEPS + 1)
            v, e, t, r = stat[:, 4:8], stat[:, 8:12], stat[:, 12:16], stat[:, 16:20]
            for k, f in enumerate((lambda: nc.vector.tensor_tensor(t, e, e, ALU.mult),
                                   lambda: nc.vector.tensor_tensor(t, t, v, ALU.mult),
                                   lambda: nc.vector.tensor_scalar(t, t, -0.5, 1.5, ALU.mult, ALU.add),
                                   lambda: nc.vector.tensor_tensor(r, e, t, ALU.mult))):
                f().then_inc(s_dve, 1)
                dve.wait_ge(s_dve, base + k + 1)
            dve.wait_ge(s_load, NLOADS + 16)
            for k in range(TILES):
                nc.vector.scalar_tensor_tensor(out=x_all[:, k, :], in0=x_all[:, k, :], scalar=stat[:, 16 + k:17 + k],
                                               in1=ffn_gain[:, 0, :], op0=ALU.mult, op1=ALU.mult).then_inc(s_fin, 1)


def shape_constants():
    k = np.zeros((P, KW), np.float32)
    k[:, K_ID:K_ID + P] = np.eye(P, dtype=np.float32)
    s = np.arange(897)[None, :] - (TILES - 1) * P
    k[:, K_MASK:K_MASK + 897] = np.where(s <= np.arange(P)[:, None], 0.0, NEG)
    k[:, K_LT:K_LT + P] = np.triu(np.ones((P, P), np.float32))
    k[:, K_IOTA:K_IOTA + TOPK] = np.arange(TOPK)
    half = ROPE // 2
    inv = (1.0 / (np.float32(10000.0) ** (np.arange(half, dtype=np.float32) / np.float32(half)))).astype(np.float32)
    ang = np.arange(SEQ, dtype=np.float32)[:, None] * inv[None, :]
    cs = np.concatenate([np.cos(ang), np.sin(ang)], axis=1).astype(np.float32)
    k[:, K_ROPE:] = cs.reshape(TILES, P, ROPE).transpose(1, 0, 2).reshape(P, TILES * ROPE)
    return k


def kernel(**inputs):
    import concourse.bacc as _bacc
    from concourse.bass_utils import run_bass_kernel_spmd as _run

    def parts(a):
        a = np.asarray(a)
        return np.ascontiguousarray(a.reshape(a.shape[0], -1, P).transpose(2, 0, 1))

    i = {k: np.asarray(v) for k, v in inputs.items()}
    data = {
        "x": i["x"], "w_in": i["w_in"], "fgate_b": i["fgate_b"], "attn_gT": parts(i["attn_norm_g"]),
        "lat_gT": parts(np.concatenate([i["mla_q_norm_g"], i["mla_kv_norm_g"]], axis=1)),
        "out_gT": parts(np.concatenate([i["out_norm_fox"], i["out_norm_mla"], i["out_norm_sb"]], axis=1)),
        "ffn_g": i["ffn_norm_g"], "final_g": i["final_norm_g"], "w_uq": i["w_uq"], "w_ukv": i["w_ukv"],
        "w_out": i["w_out"], "w_q": i["peer_w_query"],
        "keys_T": np.stack([i["peer_keys1"], i["peer_keys2"]], axis=1).transpose(3, 0, 1, 2),
        "u": i["peer_u"].reshape(DEPTH * EXPERTS, D), "v": i["peer_v"].reshape(DEPTH * EXPERTS, D),
        "consts": shape_constants(),
    }
    nc = _bacc.Bacc("TRN2", target_bir_lowering=False, num_devices=1)
    arrays, args = {}, []
    for name, a in data.items():
        a = np.ascontiguousarray(a)
        arrays[f"in_{name}_dram"] = a
        args.append(nc.dram_tensor(f"in_{name}_dram", a.shape, mybir.dt.from_np(a.dtype), kind="ExternalInput").ap())
    out = nc.dram_tensor("out_0_dram", (1, SEQ, D), F32, kind="ExternalOutput").ap()
    trunk(nc, *args, out)
    r = _run(nc, [arrays], core_ids=[0])
    return r.results[0]["out_0_dram"]
```

```python
from contextlib import ExitStack

import numpy as np

import concourse.bass as bass
from concourse import mybir

F32 = mybir.dt.float32
BF16 = mybir.dt.bfloat16
U32 = mybir.dt.uint32
ALU = mybir.AluOpType
ACT = mybir.ActivationFunctionType
AX = mybir.AxisListType

P = 128
D = 1024
SEQ = 512
DEPTH = 2
TILES = SEQ // P
STEPS = DEPTH * TILES
KC = D // P
HD = 64
FH, MH, SH = 6, 4, 6
HEADS = FH + MH + SH
FW, MW, SW = FH * HD, MH * HD, SH * HD
QR, KR = 256, 128
NOPE, ROPE = 64, 32
MD = NOPE + ROPE
EPS = 1e-6
NEG = -1e30
GONE = -3.0e38

PH = 8
NK = 128
TOPK = 16
EXPERTS = NK * NK
PICKS = PH * TOPK

C_FQ, C_FK, C_FV, C_FL = 0, FW, 2 * FW, 3 * FW
C_CQ = C_FL + FH
C_KR = C_CQ + QR + KR
C_SQ = C_KR + ROPE
C_SK, C_SV = C_SQ + SW, C_SQ + 2 * SW

WMAX = 384
BLOCKS = ([("in", c, WMAX) for c in (C_FQ, C_FK, C_FV, C_CQ, C_SQ, C_SK, C_SV)]
          + [("out", c, min(WMAX, D - c)) for c in range(0, D, WMAX)]
          + [("q", g * D + c, min(WMAX, D - c)) for g in range(2) for c in range(0, D, WMAX)])
NB = len(BLOCKS)
WSLOTS = 2
BLOCK_FILLS = ["fq", "fk", "fv", "cc", "sq", "sk", "sv", "wo0", "wo1", "wo2"] + [f"wq{i}" for i in range(6)]
assert NB % WSLOTS == 0

K_ID, K_MASK, K_LT, K_IOTA, K_ROPE = 0, 128, 128 + 897, 256 + 897, 272 + 897
KW = K_ROPE + TILES * 2 * (ROPE // 2)


def FIRST(n):
    return isinstance(n, int) and n == 0


def BLOCKS_SEEN(n):
    return 1 if FIRST(n) else TILES


R = 8
G = 4
VE = 1
PE = G - VE
GROUPS = PICKS // G
HALF = PICKS // 2
ITS = GROUPS // 2

HEAD_POINTS = [1, 3, 5, 7, 9, 10, 11, 12, 13, 14, 15]
POINTS = (["norm", "fk", "fv", "cc", "sk", "sv", "cum", "kvup"]
          + [f"head{i}" for i in HEAD_POINTS] + ["y", "z", "wo", "ffn"]
          + ["g0a", "g0b", "g0c", "g0d", "g1a", "g1b", "g1c", "g1d"])
assert len(POINTS) == GROUPS - 1, len(POINTS)


class Places:

    def __init__(self):
        self.i = 0

    def next(self, label):
        assert POINTS[self.i % len(POINTS)] == label, (POINTS[self.i % len(POINTS)], label)
        self.i += 1
        return (self.i - 1) % len(POINTS) + 1


class Ring:

    def __init__(self, bufs, fills):
        self.bufs = bufs
        self.labels = [x for x, _ in fills]
        self.by = [e for _, e in fills]
        self.per = {e: self.by.count(e) for e in "av"}

    def slot(self, label):
        return self.labels.index(label) % self.bufs

    def full(self, n, label):
        return n * len(self.labels) + self.labels.index(label) + 1

    def done(self, n, label):
        i = self.labels.index(label)
        return n * self.per[self.by[i]] + self.by[:i].count(self.by[i]) + 1

    def before(self, n, label):
        i = self.labels.index(label) - self.bufs
        return None if i < 0 else (self.by[i], self.done(n, self.labels[i]))


PA = Ring(2, [("fq", "a"), ("fk", "a"), ("fv", "a"), ("cc", "v"), ("kf", "v"), ("sq", "a"), ("sk", "a"),
              ("sv", "a"), ("cum", "v"), ("qup", "v"), ("kvup", "a")]
          + [(f"s{i}", "v") for i in range(HEADS)] + [(f"wo{i}", "v") for i in range(3)]
          + [(f"wq{i}", "a") for i in range(6)])
PB = Ring(2, [("hT0", "v"), ("hT1", "v"), ("ncT", "v"), ("cqT", "v"), ("qTm", "a"), ("kTm", "a")]
          + [(f"p{i}", "a") for i in range(HEADS)]
          + [("yT0", "v"), ("yT1", "v"), ("gT0", "a"), ("gT1", "a")])
PY = Ring(1, [("y", "v"), ("ks0", "a"), ("ks1", "a")])

DVE_LINKS = 95
ACT_LINKS = 20


def trunk(nc, x_d, w_in, w_in_kf, fgate_b, attn_gT, lat_gT, out_gT, ffn_g, final_g, w_uq, w_ukv, w_out,
          w_q, keys_T, u_d, v_d, consts_d, out_d):
    with ExitStack() as ctx:
        def sb(name, shape, dt=F32):
            return ctx.enter_context(nc.sbuf_tensor(name, shape, dt))

        def sem(name):
            return ctx.enter_context(nc.semaphore(name))

        x_all = sb("x_all", [P, TILES, D])
        u_ring = sb("u_ring", [P, R, D])
        v_ring = sb("v_ring", [P, R, D])
        h = sb("h", [P, D])
        hT = sb("hT", [P, KC, P])
        h_dot = sb("h_dot", [P, D])
        kT_fox = sb("kT_fox", [P, FH // 2, SEQ])
        kT_sb = sb("kT_sb", [P, SH // 2, SEQ])
        kT_mla = sb("kT_mla", [MD, MH, SEQ])
        v_fox = sb("v_fox", [P, TILES, FW])
        v_sb = sb("v_sb", [P, TILES, SW])
        v_mla = sb("v_mla", [P, TILES, MW])
        qT_fox = sb("qT_fox", [P, FH // 2, P])
        qT_sb = sb("qT_sb", [P, SH // 2, P])
        qT_mla = sb("qT_mla", [MD, MH, P])
        ffn_gain = sb("ffn_gain", [P, DEPTH, D])
        gT_attn = sb("gT_attn", [P, DEPTH, KC])
        gT_out = sb("gT_out", [P, DEPTH, KC])
        gT_lat = sb("gT_lat", [P, DEPTH, 3])
        gate_b = sb("gate_b", [P, DEPTH, FH])
        w_uq_sb = sb("w_uq_sb", [P, DEPTH, 2, MH * MD])
        w_ukv_sb = sb("w_ukv_sb", [P, DEPTH, MH * 2 * HD])
        keys_sb = sb("keys_sb", [P, DEPTH, 2, NK])
        consts = sb("consts", [P, KW])
        w_ring = sb("w_ring", [P, WSLOTS, KC, WMAX])
        w_kf = sb("w_kf", [P, KC, ROPE + FH])
        mask = sb("mask", [P, SEQ + 1])
        scr = sb("scr", [P, 6, SEQ])
        c_all = sb("c_all", [P, TILES + 1, FH])
        c_cur = sb("c_cur", [P, FH])
        ncT = sb("ncT", [FH, SEQ])
        fl = sb("fl", [P, 4, FH])
        stat = sb("stat", [P, 32])
        rsum = sb("rsum", [P, HEADS])
        rinv = sb("rinv", [P, HEADS])
        nmax = sb("nmax", [P, HEADS])
        top = sb("top", [P, 8, TOPK])
        top_i = sb("top_i", [P, 8, TOPK], U32)
        top_f = sb("top_f", [P, 8, TOPK])
        best = sb("best", [P, PH, TOPK])
        pos = sb("pos", [P, 4, TOPK], U32)
        gsum = sb("gsum", [P, 2, PH])
        ids = sb("ids", [P, 2 * PICKS], U32)
        gates = sb("gates", [P, 2 * PICKS])
        ids_f = sb("ids_f", [P, PICKS])
        layer_off = sb("layer_off", [P, DEPTH])
        stage_u = sb("stage_u", [P, R], U32)
        stage_v = sb("stage_v", [P, R], U32)
        dots = sb("dots", [P, R])
        gel = sb("gel", [P, R])
        coef = sb("coef", [P, R])
        diag = sb("diag", [P, PE, P])
        zero_bf = sb("zero_bf", [32, SEQ], BF16)

        pos_f = qT_fox[:, 0, :].rearrange("p (a n) -> p a n", a=2)
        key_f = qT_fox[:, 1, :].rearrange("p (a n) -> p a n", a=2)
        pos_h = qT_fox[:, 2, :].bitcast(U32).rearrange("p (a n) -> p a n", a=2)
        lat = scr[:, 3, 0:QR + KR]
        latT = scr[:, 5, 0:3 * P].rearrange("p (a n) -> p a n", n=P)
        sc = scr[:, 0:2, :]
        pr = scr[:, 2:4, :]
        pt = scr[:, 4:6, :]
        q_rows = scr[:, 0, 0:(MH + 1) * MD].rearrange("p (h d) -> p h d", d=MD)
        rope_a = scr[:, 1, 0:(MH + 1) * ROPE].rearrange("p (h k d) -> p h k d", h=MH + 1, k=2)
        rope_b = scr[:, 1, 256:256 + (MH + 1) * ROPE].rearrange("p (h k d) -> p h k d", h=MH + 1, k=2)
        k_rows = scr[:, 2, 0:MH * MD].rearrange("p (h d) -> p h d", d=MD)
        key_s = scr[:, 0:2, :].rearrange("p a (b k) -> p (a b) k", k=NK)
        cand = scr[:, 2:4, :].rearrange("p a (b k) -> p (a b) k", k=TOPK * TOPK)
        qT_peer = scr[:, 4:6, :].rearrange("p a (b k) -> p (a b) k", k=P)

        ident = consts[:, K_ID:K_ID + P]
        low_tri = consts[:, K_LT:K_LT + P]
        iota16 = consts[:, K_IOTA:K_IOTA + TOPK]

        acc = ctx.enter_context(nc.psum_tensor("acc", [P, D], F32))
        pa = ctx.enter_context(nc.psum_tensor("pa", [P, 2, SEQ], F32))
        pb = ctx.enter_context(nc.psum_tensor("pb", [P, 2, SEQ], F32))
        yp = ctx.enter_context(nc.psum_tensor("yp", [P, D], F32))

        s_first = sem("s_first")
        s_load = sem("s_load")
        s_zero = sem("s_zero")
        s_w = [sem(f"s_w{i}") for i in range(WSLOTS)]
        s_wkf = sem("s_wkf")
        pa_full, pb_full, py_full = sem("pa_full"), sem("pb_full"), sem("py_full")
        pa_free = {e: sem(f"pa_free_{e}") for e in "av"}
        pb_free = {e: sem(f"pb_free_{e}") for e in "av"}
        py_free = {e: sem(f"py_free_{e}") for e in "av"}
        s_dve, s_act = sem("s_dve"), sem("s_act")
        s_past = {e: sem(f"s_past_{e}") for e in ("pe", "act", "dve", "pool")}
        s_ss = sem("s_ss")
        s_ln = sem("s_ln")
        s_var = sem("s_var")
        s_h = sem("s_h")
        s_fz = sem("s_fz")
        s_fl = sem("s_fl")
        s_logf = sem("s_logf")
        s_ccur = sem("s_ccur")
        s_qr = sem("s_qr")
        s_kr = sem("s_kr")
        s_knope = sem("s_knope")
        s_mask = sem("s_mask")
        s_abs = sem("s_abs")
        s_sp = sem("s_sp")
        s_arg = sem("s_arg")
        s_p = sem("s_p")
        s_pv = sem("s_pv")
        s_y = sem("s_y")
        s_keys = sem("s_keys")
        s_keysfree = sem("s_keysfree")
        s_best = sem("s_best")
        s_bexp = sem("s_bexp")
        s_ids = sem("s_ids")
        s_stage_u = sem("s_stage_u")
        s_stage_v = sem("s_stage_v")
        s_u = [sem(f"s_u{i}") for i in range(R)]
        s_v = [sem(f"s_v{i}") for i in range(R)]
        s_dot = sem("s_dot")
        s_mm = sem("s_mm")
        s_axpy = sem("s_axpy")
        s_gel = sem("s_gel")
        s_coef = sem("s_coef")
        s_diag = sem("s_diag")
        s_acc = sem("s_acc")
        s_acc_free = sem("s_acc_free")
        s_fin = sem("s_fin")
        s_out = sem("s_out")

        block = ctx.enter_context(nc.Block())

        def bc(ap2, axis, count):
            return ap2.unsqueeze(axis).to_broadcast(
                [*ap2.shape[:axis], count, *ap2.shape[axis:]])

        LOADS = []

        @block.sync
        def _(sp):
            def load(dst, src):
                sp.dma_start(dst, src).then_inc(s_load, 16)
                LOADS.append(1)

            def other_loads():
                for t in range(1, TILES):
                    load(x_all[:, t, :], x_d[0, t * P:(t + 1) * P, :])
                load(gate_b[:], fgate_b.rearrange("l n -> (l n)").unsqueeze(0).to_broadcast([P, DEPTH * FH])
                     .rearrange("p (l n) -> p l n", l=DEPTH))
                load(gT_lat[:], lat_gT)
                load(w_uq_sb[:], w_uq.rearrange("l (c p) n -> p l c n", p=P))
                load(w_ukv_sb[:], w_ukv.rearrange("l p n -> p l n"))
                load(gT_out[:], out_gT)
                load(keys_sb[:], keys_T)
                load(ffn_gain[:], ffn_g.rearrange("l n -> (l n)").unsqueeze(0).to_broadcast([P, DEPTH * D])
                     .rearrange("p (l n) -> p l n", l=DEPTH))

            def weights(n):
                layer = n // TILES
                for i, (m, c, w) in enumerate(BLOCKS):
                    if i == WSLOTS and FIRST(n):
                        other_loads()
                    if i >= WSLOTS:
                        sp.wait_ge(pa_full, PA.full(n, BLOCK_FILLS[i - WSLOTS]))
                    elif not FIRST(n):
                        sp.wait_ge(pa_full, PA.full(n - 1, BLOCK_FILLS[i - WSLOTS]))
                    src = {"in": w_in, "out": w_out, "q": w_q}[m]
                    sp.dma_start(w_ring[:, i % WSLOTS, :, 0:w],
                                 src[bass.ds(layer, 1), :, c:c + w].rearrange("l (c p) n -> p (l c) n", p=P)
                                 ).then_inc(s_w[i % WSLOTS], 16)
                    if i == 0:
                        sp.dma_start(w_kf[:], w_in_kf[bass.ds(layer, 1), :, :].rearrange("l p n -> p (l n)")
                                     .rearrange("p (c n) -> p c n", c=KC)).then_inc(s_wkf, 16)
            sp.dma_start(x_all[:, 0, :], x_d[0, 0:P, :]).then_inc(s_first, 16)
            sp.dma_start(consts[:], consts_d).then_inc(s_first, 16)
            sp.dma_start(gT_attn[:], attn_gT).then_inc(s_first, 16)
            weights(0)
            with sp.Fori(1, STEPS) as n:
                weights(n)
            sp.wait_ge(s_ids, 2 * STEPS)
            sp.dma_start(ffn_gain[:, 0, :], final_g.unsqueeze(0).to_broadcast([P, D])).then_inc(s_load, 16)
            for t in range(TILES):
                sp.wait_ge(s_fin, t + 1)
                sp.dma_start(out_d[0, t * P:(t + 1) * P, :], x_all[:, t, :]).then_inc(s_out, 16)
            sp.wait_ge(s_out, 16 * TILES)

        FIRST_LOADS = 16 * 3
        NLOADS = 16 * len(LOADS)

        @block.gpsimd
        def _(pool):
            for b in (kT_fox, kT_sb, kT_mla, v_fox, v_sb, v_mla, c_all, ncT, zero_bf):
                nc.gpsimd.memset(b[:], 0.0).then_inc(s_zero, 1)
            for l in range(DEPTH):
                nc.gpsimd.memset(layer_off[:, l:l + 1], float(l * EXPERTS)).then_inc(s_zero, 1)
            def rows_of_u(m, it, q):
                pool.wait_ge(s_dot, m * PICKS + it * R + (q + 1) * G)
                pool.sem_inc(s_past["pool"], 1)
                nc.gpsimd.tensor_copy(stage_u[:, q * G:q * G + G],
                                      ids[:, bass.ds((m % 2) * PICKS + it * R + q * G, G)]).then_inc(s_stage_u, 1)
                pool.wait_ge(s_stage_u, m * GROUPS + it * 2 + q + 1)
                pool.sem_inc(s_past["pool"], 1)
                for j in range(q * G, q * G + G):
                    pool.indirect_dma_start(
                        out=u_ring[:, j, :], out_offset=None, in_=u_d,
                        in_offset=bass.IndirectOffsetOnAxis(ap=stage_u[:, j:j + 1], axis=0)).then_inc(s_u[j], 16)

            def rows_of_v(m, it, q):
                pool.wait_ge(s_mm, (m * GROUPS + it * 2 + q + 1) * PE)
                pool.wait_ge(s_axpy, (m * GROUPS + it * 2 + q + 1) * VE)
                pool.sem_inc(s_past["pool"], 1)
                nc.gpsimd.tensor_copy(stage_v[:, q * G:q * G + G],
                                      ids[:, bass.ds((m % 2) * PICKS + it * R + q * G, G)]).then_inc(s_stage_v, 1)
                pool.wait_ge(s_stage_v, m * GROUPS + it * 2 + q + 1)
                pool.sem_inc(s_past["pool"], 1)
                for j in range(q * G, q * G + G):
                    pool.indirect_dma_start(
                        out=v_ring[:, j, :], out_offset=None, in_=v_d,
                        in_offset=bass.IndirectOffsetOnAxis(ap=stage_v[:, j:j + 1], axis=0)).then_inc(s_v[j], 16)

            with pool.Fori(0, STEPS) as m:
                pool.wait_ge(s_ids, 2 * m + 1)
                pool.sem_inc(s_past["pool"], 1)
                for q in range(2):
                    rows_of_u(m, 0, q)
                for first, last in ((0, ITS // 2 - 1), (ITS // 2 - 1, ITS - 1)):
                    if first:
                        pool.wait_ge(s_ids, 2 * m + 2)
                        pool.sem_inc(s_past["pool"], 1)
                    with pool.Fori(first, last) as it:
                        for q in range(2):
                            rows_of_v(m, it, q)
                            rows_of_u(m, it + 1, q)
                for q in range(2):
                    rows_of_v(m, ITS - 1, q)

        @block.tensor
        def _(pe):
            def fill(n, ring, name, sems, label):
                b = ring.before(n, label)
                if b is not None:
                    pe.wait_ge(sems[b[0]], b[1])

            def past():
                pe.sem_inc(s_past["pe"], 1)

            def transposes(n, label, srcs, rows=P):
                fill(n, PB, "pb", pb_free, label)
                past()
                for i, s in enumerate(srcs):
                    mm = nc.tensor.transpose(pb[0:rows, PB.slot(label), i * P:(i + 1) * P], s, ident)
                return mm

            def weights(n, i):
                pe.wait_ge(s_w[i % WSLOTS], (n * (NB // WSLOTS) + i // WSLOTS + 1) * 16)

            def cols_T(n, i, label):
                w = BLOCKS[i][2]
                weights(n, i)
                fill(n, PA, "pa", pa_free, label)
                past()
                for j in range(w // P):
                    for c in range(KC):
                        mm = nc.tensor.matmul(pa[:, PA.slot(label), j * P:(j + 1) * P],
                                              w_ring[:, i % WSLOTS, c, j * P:(j + 1) * P], hT[:, c, :],
                                              start=(c == 0), stop=(c == KC - 1))
                mm.then_inc(pa_full, 1)

            def rows_of(n, i, label):
                w = BLOCKS[i][2]
                weights(n, i)
                fill(n, PA, "pa", pa_free, label)
                past()
                for c in range(KC):
                    mm = nc.tensor.matmul(pa[:, PA.slot(label), 0:w], hT[:, c, :], w_ring[:, i % WSLOTS, c, 0:w],
                                          start=(c == 0), stop=(c == KC - 1))
                mm.then_inc(pa_full, 1)

            def mixer(n):
                tile, layer = n % TILES, n // TILES
                pe.wait_ge(s_h, 4 * n + 1)
                for j in range(2):
                    transposes(n, f"hT{j}", [h[:, (4 * j + i) * P:(4 * j + i + 1) * P] for i in range(4)]
                               ).then_inc(pb_full, 1)
                pe.wait_ge(pb_free["v"], PB.done(n, "hT1"))
                cols_T(n, 0, "fq")
                rows(n, "norm")
                cols_T(n, 1, "fk")
                rows(n, "fk")
                rows_of(n, 2, "fv")
                rows(n, "fv")
                rows_of(n, 3, "cc")
                pe.wait_ge(s_wkf, 16 * (n + 1))
                fill(n, PA, "pa", pa_free, "kf")
                past()
                for c in range(KC):
                    mm = nc.tensor.matmul(pa[:, PA.slot("kf"), 0:ROPE + FH], hT[:, c, :], w_kf[:, c, :],
                                          start=(c == 0), stop=(c == KC - 1))
                mm.then_inc(pa_full, 1)
                rows(n, "cc")
                cols_T(n, 4, "sq")
                cols_T(n, 5, "sk")
                rows(n, "sk")
                rows_of(n, 6, "sv")
                pe.wait_ge(s_logf, n + 1)
                fill(n, PA, "pa", pa_free, "cum")
                past()
                nc.tensor.matmul(pa[:, PA.slot("cum"), 0:FH], low_tri, fl[:, 3, :], start=True, stop=False)
                nc.tensor.matmul(pa[:, PA.slot("cum"), 0:FH], ident[:, P - 1:P].to_broadcast([P, P]),
                                 c_all[:, bass.ds(tile, 1), :].rearrange("p a n -> p (a n)"),
                                 start=False, stop=True).then_inc(pa_full, 1)
                pe.wait_ge(s_ccur, n + 1)
                transposes(n, "ncT", [c_cur[:]], rows=FH).then_inc(pb_full, 1)
                rows(n, "sv")
                if FIRST(n):
                    pe.wait_ge(s_load, NLOADS)
                pe.wait_ge(s_h, 4 * n + 2)
                transposes(n, "cqT", [lat[:, i * P:(i + 1) * P] for i in range(3)]).then_inc(pb_full, 1)
                rows(n, "cum")
                pe.wait_ge(pb_free["v"], PB.done(n, "cqT"))
                fill(n, PA, "pa", pa_free, "qup")
                past()
                for c in range(2):
                    mm = nc.tensor.matmul(pa[:, PA.slot("qup"), 0:MH * MD], latT[:, c, :],
                                          w_uq_sb[:, bass.ds(layer, 1), c, :].rearrange("p a n -> p (a n)"),
                                          start=(c == 0), stop=(c == 1))
                mm.then_inc(pa_full, 1)
                fill(n, PA, "pa", pa_free, "kvup")
                past()
                nc.tensor.matmul(pa[:, PA.slot("kvup"), :], latT[:, 2, :],
                                 w_ukv_sb[:, bass.ds(layer, 1), :].rearrange("p a n -> p (a n)"),
                                 start=True, stop=True).then_inc(pa_full, 1)
                pe.wait_ge(s_qr, n + 1)
                transposes(n, "qTm", [q_rows[:, i, :] for i in range(MH)], rows=MD).then_inc(pb_full, 1)
                pe.wait_ge(s_kr, n + 1)
                pe.wait_ge(s_knope, n + 1)
                transposes(n, "kTm", [k_rows[:, i, :] for i in range(MH)], rows=MD).then_inc(pb_full, 1)
                rows(n, "kvup")
                pe.wait_ge(pb_free["v"], PB.done(n, "ncT"))
                pe.wait_ge(pa_free["a"], PA.done(n, "kvup"))
                pe.wait_ge(pb_free["a"], PB.done(n, "kTm"))

            def scores(n, i):
                lab = f"s{i}"
                fill(n, PA, "pa", pa_free, lab)
                past()
                w = BLOCKS_SEEN(n) * P
                o = pa[:, PA.slot(lab), 0:w]
                if i < FH:
                    r = slice(64 * (i % 2), 64 * (i % 2) + 64)
                    nc.tensor.matmul(o, qT_fox[r, i // 2, :], kT_fox[r, i // 2, 0:w], start=True, stop=False)
                    mm = nc.tensor.matmul(o, ident[0:FH, i:i + 1].to_broadcast([FH, P]), ncT[:, 0:w],
                                          start=False, stop=True)
                elif i < FH + MH:
                    mm = nc.tensor.matmul(o, qT_mla[:, i - FH, :], kT_mla[:, i - FH, 0:w], start=True, stop=True)
                else:
                    k = i - FH - MH
                    r = slice(64 * (k % 2), 64 * (k % 2) + 64)
                    mm = nc.tensor.matmul(o, qT_sb[r, k // 2, :], kT_sb[r, k // 2, 0:w], start=True, stop=True)
                mm.then_inc(pa_full, 1)

            def turn(n, i):
                pe.wait_ge(s_p, n * HEADS + i + 1)
                transposes(n, f"p{i}", [pr[:, i % 2, b * P:(b + 1) * P] for b in range(BLOCKS_SEEN(n))]
                           ).then_inc(pb_full, 1)

            def pv(n, i):
                pe.wait_ge(pb_free["a"], PB.done(n, f"p{i}"))
                past()
                for b in range(BLOCKS_SEEN(n)):
                    if i < FH:
                        v = v_fox[:, b, i * HD:(i + 1) * HD]
                    elif i < FH + MH:
                        v = v_mla[:, b, (i - FH) * HD:(i - FH + 1) * HD]
                    else:
                        v = v_sb[:, b, (i - FH - MH) * HD:(i - FH - MH + 1) * HD]
                    mm = nc.tensor.matmul(yp[:, i * HD:(i + 1) * HD], pt[:, i % 2, b * P:(b + 1) * P], v,
                                          start=(b == 0), stop=(b == BLOCKS_SEEN(n) - 1))
                mm.then_inc(s_pv, 1)

            def attention(n):
                scores(n, 0)
                for i in range(HEADS + 2):
                    if i + 1 < HEADS:
                        scores(n, i + 1)
                    early = 1 <= i <= FH + MH
                    if early:
                        turn(n, i - 1)
                    if i - 1 in HEAD_POINTS:
                        rows(n, f"head{i - 1}")
                    if not early and 1 <= i <= HEADS:
                        turn(n, i - 1)
                    if i >= 2:
                        pv(n, i - 2)

            def output(n):
                rows(n, "y")
                pe.wait_ge(s_h, 4 * n + 3)
                for j in range(2):
                    transposes(n, f"yT{j}", [h[:, (4 * j + i) * P:(4 * j + i + 1) * P] for i in range(4)]
                               ).then_inc(pb_full, 1)
                rows(n, "z")
                pe.wait_ge(pb_free["v"], PB.done(n, "yT1"))
                for j in range(3):
                    rows_of(n, 7 + j, f"wo{j}")
                rows(n, "wo")

            def routing(n):
                layer = n // TILES
                pe.wait_ge(s_h, 4 * n + 4)
                for j in range(2):
                    transposes(n, f"gT{j}", [h[:, (4 * j + i) * P:(4 * j + i + 1) * P] for i in range(4)]
                               ).then_inc(pb_full, 1)
                rows(n, "ffn")
                pe.wait_ge(pb_free["a"], PB.done(n, "gT1"))

                def key_scores(g):
                    pe.wait_ge(pa_free["a"], PA.done(n, f"wq{3 * g + 2}"))
                    fill(n, PY, "py", py_free, f"ks{g}")
                    past()
                    for k in range(8):
                        mm = nc.tensor.matmul(yp[:, k * NK:(k + 1) * NK], qT_peer[:, k, :],
                                              keys_sb[:, bass.ds(layer, 1), k % 2, :].rearrange("p a n -> p (a n)"),
                                              start=True, stop=True)
                    mm.then_inc(py_full, 1)

                cols_T(n, 10, "wq0")
                rows(n, "g0a")
                cols_T(n, 11, "wq1")
                rows(n, "g0b")
                cols_T(n, 12, "wq2")
                key_scores(0)
                cols_T(n, 13, "wq3")
                rows(n, "g0c")
                cols_T(n, 14, "wq4")
                rows(n, "g0d")
                cols_T(n, 15, "wq5")
                rows(n, "g1a")
                key_scores(1)
                for p in "bcd":
                    rows(n, f"g1{p}")
                for ring, sems in ((PA, pa_free), (PB, pb_free), (PY, py_free)):
                    for e in "av":
                        pe.wait_ge(sems[e], (n + 1) * ring.per[e])

            def sum_start(m):
                pe.wait_ge(s_acc_free, m + 1)
                past()
                for c in range(2):
                    nc.tensor.matmul(acc[:, c * 512:c * 512 + 512], zero_bf[:, 0:P], zero_bf[:, :],
                                     start=True, stop=False)

            def sum_rows(m, it, q):
                for i in range(PE):
                    j = q * G + i
                    pe.wait_ge(s_diag, (m * GROUPS + it * 2 + q) * PE + i + 1)
                    pe.wait_ge(s_v[j], (m * ITS + it + 1) * 16)
                    for c in range(2):
                        mm = nc.tensor.matmul(acc[:, c * 512:c * 512 + 512], diag[:, i, :],
                                              v_ring[:, j, c * 512:c * 512 + 512], start=False, stop=False)
                    mm.then_inc(s_mm, 1)

            def sum_end():
                for c in range(2):
                    mm = nc.tensor.matmul(acc[:, c * 512:c * 512 + 512], zero_bf[:, 0:P], zero_bf[:, :],
                                          start=False, stop=True)
                mm.then_inc(s_acc, 1)

            places = Places()

            def rows(n, label):
                if FIRST(n):
                    return
                p = places.next(label)
                if p == 1:
                    sum_start(n - 1)
                sum_rows(n - 1, *divmod(p - 1, 2))

            def last_rows(n):
                if not FIRST(n):
                    sum_rows(n - 1, *divmod(GROUPS - 1, 2))
                    sum_end()

            pe.wait_ge(s_first, FIRST_LOADS)
            pe.wait_ge(s_zero, 9 + DEPTH)
            pe.sem_inc(s_mm, 2 * PE)

            def step(n):
                mixer(n)
                attention(n)
                output(n)
                routing(n)
                last_rows(n)

            step(0)
            with pe.Fori(1, STEPS) as n:
                step(n)
            sum_start(STEPS - 1)
            with pe.Fori(0, ITS) as it:
                for q in range(2):
                    sum_rows(STEPS - 1, it, q)
            sum_end()

        @block.scalar
        def _(act):
            links = [0]

            def link(n, ins):
                links[0] += 1
                ins.then_inc(s_act, 1)
                act.wait_ge(s_act, n * ACT_LINKS + links[0])

            def past():
                act.sem_inc(s_past["act"], 1)

            def take(n, ring, full, label):
                act.wait_ge(full, ring.full(n, label))
                past()

            def squares(src, dst, junk):
                return nc.scalar.activation(junk, src, ACT.Square, accum_out=dst)

            def rsqrt(n, k, cols, dst):
                act.wait_ge(s_var, 4 * n + k)
                link(n, nc.scalar.activation(dst, cols, ACT.Ln))
                nc.scalar.activation(dst, dst, ACT.Exp, scale=-0.5).then_inc(s_ln, 1)

            def norm_squares(n, tile):
                if not (isinstance(n, int) and n < 2):
                    act.wait_ge(s_acc_free, n - 1)
                    past()
                squares(x_all[:, bass.ds(tile, 1), :].rearrange("p a n -> p (a n)"), stat[:, 0:1],
                        scr[:, 4:6, :].rearrange("p a n -> p (a n)")).then_inc(s_ss, 1)

            def mixer(n):
                tile, layer = n % TILES, n // TILES
                past()
                nc.scalar.copy(mask[:], consts[:, bass.ds(K_MASK + (TILES - 1 - tile) * P, SEQ + 1)]).then_inc(s_mask, 1)
                rows(n, "norm")
                take(n, PA, pa_full, "fq")
                nc.scalar.activation(qT_fox[:].rearrange("p a n -> p (a n)"), pa[:, PA.slot("fq"), 0:FW], ACT.Copy,
                                     scale=HD ** -0.5).then_inc(pa_free["a"], 1)
                take(n, PA, pa_full, "fk")
                nc.scalar.copy(kT_fox[:, :, bass.ds(tile * P, P)],
                               pa[:, PA.slot("fk"), 0:FW].rearrange("p (a n) -> p a n", n=P)).then_inc(pa_free["a"], 1)
                rows(n, "fk")
                take(n, PA, pa_full, "fv")
                nc.scalar.copy(v_fox[:, bass.ds(tile, 1), :].rearrange("p a n -> p (a n)"),
                               pa[:, PA.slot("fv"), 0:FW]).then_inc(pa_free["a"], 1)
                rows(n, "fv")
                rows(n, "cc")
                act.wait_ge(s_fz, n + 1)
                link(n, nc.scalar.activation(fl[:, 1, :], fl[:, 0, :], ACT.Abs))
                link(n, nc.scalar.activation(fl[:, 1, :], fl[:, 1, :], ACT.Exp, scale=-1.0))
                nc.scalar.activation(fl[:, 1, :], fl[:, 1, :], ACT.Ln, bias=1.0).then_inc(s_fl, 1)
                link(n, squares(lat[:, 0:QR], stat[:, 1:2], scr[:, 4, 0:QR]))
                squares(lat[:, QR:QR + KR], stat[:, 2:3], scr[:, 4, 256:256 + KR]).then_inc(s_ss, 1)
                rsqrt(n, 2, stat[:, 5:7], stat[:, 9:11])
                take(n, PA, pa_full, "sq")
                nc.scalar.activation(qT_sb[:].rearrange("p a n -> p (a n)"), pa[:, PA.slot("sq"), 0:SW], ACT.Copy,
                                     scale=HD ** -0.5).then_inc(pa_free["a"], 1)
                take(n, PA, pa_full, "sk")
                nc.scalar.copy(kT_sb[:, :, bass.ds(tile * P, P)],
                               pa[:, PA.slot("sk"), 0:SW].rearrange("p (a n) -> p a n", n=P)).then_inc(pa_free["a"], 1)
                rows(n, "sk")
                take(n, PA, pa_full, "sv")
                nc.scalar.copy(v_sb[:, bass.ds(tile, 1), :].rearrange("p a n -> p (a n)"),
                               pa[:, PA.slot("sv"), 0:SW]).then_inc(pa_free["a"], 1)
                rows(n, "sv")
                rows(n, "cum")
                take(n, PA, pa_full, "kvup")
                kv = pa[:, PA.slot("kvup"), :].rearrange("p (h d) -> p h d", d=2 * HD)
                nc.scalar.copy(k_rows[:, :, 0:NOPE], kv[:, :, 0:NOPE]).then_inc(s_knope, 1)
                nc.scalar.copy(v_mla[:, bass.ds(tile, 1), :].rearrange("p a (h d) -> p (a h) d", d=HD),
                               kv[:, :, NOPE:2 * HD]).then_inc(pa_free["a"], 1)
                take(n, PB, pb_full, "qTm")
                nc.scalar.activation(qT_mla[:].rearrange("p a n -> p (a n)"), pb[0:MD, PB.slot("qTm"), :], ACT.Copy,
                                     scale=MD ** -0.5).then_inc(pb_free["a"], 1)
                take(n, PB, pb_full, "kTm")
                nc.scalar.copy(kT_mla[:, :, bass.ds(tile * P, P)],
                               pb[0:MD, PB.slot("kTm"), :].rearrange("p (a n) -> p a n", n=P)
                               ).then_inc(pb_free["a"], 1)
                rows(n, "kvup")

            def first(n, i):
                act.wait_ge(pa_free["v"], PA.done(n, f"s{i}"))
                past()
                w = BLOCKS_SEEN(n) * P
                s, p = sc[:, i % 2, 0:w], pr[:, i % 2, 0:w]
                if i < FH + MH:
                    nc.scalar.activation(p, s, ACT.Exp, scale=-1.0, bias=nmax[:, i:i + 1],
                                         accum_out=rsum[:, i:i + 1]).then_inc(s_p, 1)
                else:
                    act.wait_ge(s_abs, n * SH + i - FH - MH + 1)
                    link(n, nc.scalar.activation(p, p, ACT.Exp))
                    nc.scalar.activation(p, p, ACT.Ln, bias=1.0).then_inc(s_sp, 1)

            def second(n, i):
                if i >= FH + MH:
                    act.wait_ge(s_arg, n * SH + i - FH - MH + 1)
                    p = pr[:, i % 2, 0:BLOCKS_SEEN(n) * P]
                    nc.scalar.activation(p, p, ACT.Exp).then_inc(s_p, 1)

            def turned(n, i):
                take(n, PB, pb_full, f"p{i}")
                if i >= 2:
                    act.wait_ge(s_pv, n * HEADS + i - 1)
                    past()
                w = BLOCKS_SEEN(n) * P
                nc.scalar.copy(pt[:, i % 2, 0:w], pb[:, PB.slot(f"p{i}"), 0:w]).then_inc(pb_free["a"], 1)

            def attention(n):
                for i in range(HEADS + 1):
                    if i < HEADS:
                        first(n, i)
                    if 1 <= i <= HEADS:
                        second(n, i - 1)
                        turned(n, i - 1)
                    if i in HEAD_POINTS:
                        rows(n, f"head{i}")

            def output(n):
                rows(n, "y")
                act.wait_ge(s_y, n + 1)
                past()
                for k, (a, b) in enumerate(((0, FW), (FW, FW + MW), (FW + MW, D))):
                    link(n, squares(h[:, a:b], stat[:, 12 + k:13 + k], scr[:, 0:2, :].rearrange("p a n -> p (a n)")[:, a:b]))
                act.sem_inc(s_ss, 1)
                rsqrt(n, 3, stat[:, 16:19], stat[:, 20:23])
                rows(n, "z")
                rows(n, "wo")
                act.wait_ge(pa_free["v"], n * PA.per["v"] + PA.per["v"])
                past()
                squares(x_all[:, bass.ds(n % TILES, 1), :].rearrange("p a n -> p (a n)"), stat[:, 0:1],
                        scr[:, 4:6, :].rearrange("p a n -> p (a n)")).then_inc(s_ss, 1)
                rsqrt(n, 4, stat[:, 4:5], stat[:, 8:9])
                rows(n, "ffn")

            def routing(n):
                for j in range(2):
                    take(n, PB, pb_full, f"gT{j}")
                    nc.scalar.copy(hT[:, 4 * j:4 * j + 4, :].rearrange("p a n -> p (a n)"), pb[:, PB.slot(f"gT{j}"), :]
                                   ).then_inc(pb_free["a"], 1)

                def queries(i):
                    w = BLOCKS[10 + i][2]
                    take(n, PA, pa_full, f"wq{i}")
                    nc.scalar.copy(qT_peer[:, 3 * (i % 3):3 * (i % 3) + w // P, :].rearrange("p a n -> p (a n)"),
                                   pa[:, PA.slot(f"wq{i}"), 0:w]).then_inc(pa_free["a"], 1)

                def key_scores(g):
                    act.wait_ge(py_full, 2 * n + g + 1)
                    past()
                    if g == 1:
                        act.wait_ge(s_keysfree, 2 * n + 1)
                        past()
                    for j in range(2):
                        link(n, nc.scalar.copy(key_s[:, 4 * j:4 * j + 4, :].rearrange("p a n -> p (a n)"),
                                               yp[:, j * 512:j * 512 + 512]))
                    act.sem_inc(s_keys, 1)
                    act.sem_inc(py_free["a"], 1)

                queries(0)
                rows(n, "g0a")
                queries(1)
                rows(n, "g0b")
                queries(2)
                key_scores(0)
                queries(3)
                rows(n, "g0c")
                queries(4)
                rows(n, "g0d")
                queries(5)
                rows(n, "g1a")
                key_scores(1)
                rows(n, "g1b")
                rows(n, "g1c")
                rows(n, "g1d")
                act.wait_ge(s_best, n + 1)
                nc.scalar.activation(best[:], best[:], ACT.Exp).then_inc(s_bexp, 1)

            def weigh(m, it, q):
                k = m * GROUPS + it * 2 + q
                act.wait_ge(s_dot, m * PICKS + it * R + (q + 1) * G + R)
                nc.scalar.activation(gel[:, q * G:q * G + G], dots[:, q * G:q * G + G], ACT.Gelu
                                     ).then_inc(s_gel, 1)
                act.wait_ge(s_gel, k + 1 + 2)
                act.wait_ge(s_axpy, (k + 1) * VE)
                past()
                for j in range(q * G, q * G + G):
                    ins = nc.scalar.activation(coef[:, j:j + 1], gel[:, j:j + 1], ACT.Copy,
                                               scale=gates[:, bass.ds((m % 2) * PICKS + it * R + j, 1)])
                ins.then_inc(s_coef, 1)
                act.wait_ge(s_coef, k + 1)
                for i in range(PE):
                    act.wait_ge(s_mm, (k + 1) * PE + i + 1)
                    nc.scalar.activation(diag[:, i, :], ident, ACT.Copy, scale=coef[:, q * G + i:q * G + i + 1]
                                         ).then_inc(s_diag, 1)

            places = Places()

            def rows(n, label):
                if FIRST(n):
                    return
                p = places.next(label)
                weigh(n - 1, *divmod(p - 1, 2))

            act.wait_ge(s_first, FIRST_LOADS)
            act.wait_ge(s_zero, 9 + DEPTH)

            def step(n):
                mixer(n)
                attention(n)
                output(n)
                routing(n)
                assert links[0] == ACT_LINKS, links
                norm_squares(n + 1, (n + 1) % TILES)
                if not FIRST(n):
                    weigh(n - 1, *divmod(GROUPS - 1, 2))
                links[0] = 0
                rsqrt(n + 1, 1, stat[:, 4:5], stat[:, 8:9])

            norm_squares(0, 0)
            rsqrt(0, 1, stat[:, 4:5], stat[:, 8:9])
            act.wait_ge(s_load, NLOADS)
            step(0)
            with act.Fori(1, STEPS) as n:
                step(n)

            def final_norm(t):
                act.wait_ge(s_acc_free, STEPS - TILES + t + 2)
                squares(x_all[:, t, :], stat[:, 0:1], scr[:, 4:6, :].rearrange("p a n -> p (a n)")).then_inc(s_ss, 1)
                rsqrt(STEPS, 1 + t, stat[:, 4:5], stat[:, 8:9])

            for t in range(1, TILES - 1):
                final_norm(t)
            act.wait_ge(s_ids, 2 * STEPS)
            act.sem_inc(s_past["act"], 1)
            with act.Fori(0, ITS) as it:
                for q in range(2):
                    weigh(STEPS - 1, it, q)
            final_norm(TILES - 1)

        @block.vector
        def _(dve):
            links = [0]

            def link(n, ins):
                links[0] += 1
                ins.then_inc(s_dve, 1)
                dve.wait_ge(s_dve, n * DVE_LINKS + links[0])

            def past():
                dve.sem_inc(s_past["dve"], 1)

            def take(n, ring, full, label):
                dve.wait_ge(full, ring.full(n, label))
                past()

            def refine(n, k, var, est, dst, tmp):
                dve.wait_ge(s_ln, 4 * n + k)
                link(n, nc.vector.tensor_tensor(tmp, est, est, ALU.mult))
                link(n, nc.vector.tensor_tensor(tmp, tmp, var, ALU.mult))
                link(n, nc.vector.tensor_scalar(tmp, tmp, -0.5, 1.5, ALU.mult, ALU.add))
                link(n, nc.vector.tensor_tensor(dst, est, tmp, ALU.mult))

            def variance(dst, src, width):
                return nc.vector.tensor_scalar(dst, src, 1.0 / width, EPS, ALU.mult, ALU.add)

            def x_tile(n):
                return x_all[:, bass.ds(n % TILES, 1), :].rearrange("p a n -> p (a n)")

            def norm(n):
                dve.wait_ge(s_ss, 4 * n + 1)
                variance(stat[:, 4:5], stat[:, 0:1], D).then_inc(s_var, 1)
                refine(n, 1, stat[:, 4:5], stat[:, 8:9], stat[:, 30:31], stat[:, 31:32])
                past()
                nc.vector.tensor_scalar(h[:], x_tile(n), stat[:, 30:31], None, ALU.mult).then_inc(s_h, 1)

            def mixer(n):
                tile, layer = n % TILES, n // TILES

                def turned(labels, gT):
                    for j, lab in enumerate(labels):
                        take(n, PB, pb_full, lab)
                        nc.vector.tensor_tensor(
                            hT[:, 4 * j:4 * j + 4, :], pb[:, PB.slot(lab), :].rearrange("p (a n) -> p a n", n=P),
                            bc(gT[:, bass.ds(layer, 1), 4 * j:4 * j + 4].rearrange("p a n -> p (a n)"), 2, P),
                            ALU.mult).then_inc(pb_free["v"], 1)

                turned(["hT0", "hT1"], gT_attn)
                if FIRST(n):
                    dve.wait_ge(s_load, NLOADS)
                rows(n, "norm")
                rows(n, "fk")
                rows(n, "fv")
                take(n, PA, pa_full, "cc")
                nc.vector.tensor_copy(lat, pa[:, PA.slot("cc"), 0:QR + KR]).then_inc(pa_free["v"], 1)
                take(n, PA, pa_full, "kf")
                nc.vector.tensor_copy(q_rows[:, MH, NOPE:MD], pa[:, PA.slot("kf"), 0:ROPE])
                nc.vector.tensor_tensor(fl[:, 0, :], pa[:, PA.slot("kf"), ROPE:ROPE + FH],
                                        gate_b[:, bass.ds(layer, 1), :].rearrange("p a n -> p (a n)"),
                                        ALU.add).then_inc(pa_free["v"], 1)
                dve.wait_ge(pa_free["v"], n * PA.per["v"] + 2)
                dve.sem_inc(s_fz, 1)
                rows(n, "cc")
                dve.wait_ge(s_fl, n + 1)
                nc.vector.scalar_tensor_tensor(out=fl[:, 3, :], in0=fl[:, 0, :], scalar=0.0, in1=fl[:, 1, :],
                                               op0=ALU.min, op1=ALU.subtract).then_inc(s_logf, 1)
                dve.wait_ge(s_ss, 4 * n + 2)
                link(n, variance(stat[:, 5:6], stat[:, 1:2], QR))
                variance(stat[:, 6:7], stat[:, 2:3], KR).then_inc(s_var, 1)
                refine(n, 2, stat[:, 5:7], stat[:, 9:11], stat[:, 26:28], stat[:, 28:30])
                link(n, nc.vector.tensor_scalar(lat[:, 0:QR], lat[:, 0:QR], stat[:, 26:27], None, ALU.mult))
                nc.vector.tensor_scalar(lat[:, QR:], lat[:, QR:], stat[:, 27:28], None, ALU.mult).then_inc(s_h, 1)
                rows(n, "sk")
                rows(n, "sv")
                take(n, PA, pa_full, "cum")
                nc.vector.tensor_copy(c_cur[:], pa[:, PA.slot("cum"), 0:FH]).then_inc(s_ccur, 1)
                nc.vector.tensor_copy(c_all[:, bass.ds(tile + 1, 1), :].rearrange("p a n -> p (a n)"),
                                      pa[:, PA.slot("cum"), 0:FH]).then_inc(pa_free["v"], 1)
                take(n, PB, pb_full, "ncT")
                nc.vector.tensor_scalar(ncT[:, bass.ds(tile * P, P)], pb[0:FH, PB.slot("ncT"), 0:P], -1.0, None,
                                        ALU.mult).then_inc(pb_free["v"], 1)
                take(n, PB, pb_full, "cqT")
                nc.vector.tensor_tensor(
                    latT, pb[:, PB.slot("cqT"), 0:3 * P].rearrange("p (a n) -> p a n", n=P),
                    bc(gT_lat[:, bass.ds(layer, 1), :].rearrange("p a n -> p (a n)"), 2, P),
                    ALU.mult).then_inc(pb_free["v"], 1)
                rows(n, "cum")
                take(n, PA, pa_full, "qup")
                nc.vector.tensor_copy(q_rows[:, 0:MH, :],
                                      pa[:, PA.slot("qup"), 0:MH * MD].rearrange("p (h d) -> p h d", d=MD)
                                      ).then_inc(pa_free["v"], 1)
                dve.wait_ge(pa_free["v"], n * PA.per["v"] + 4)
                hf = ROPE // 2
                rot = q_rows[:, :, NOPE:MD].rearrange("p h (k d) -> p h k d", k=2)
                past()
                for k in range(2):
                    t = consts[:, bass.ds(tile * ROPE + K_ROPE, hf)]
                    link(n, nc.vector.tensor_tensor(rope_a[:, :, k, :], rot[:, :, k, :], bc(t, 1, MH + 1), ALU.mult))
                    t = consts[:, bass.ds(tile * ROPE + K_ROPE + hf, hf)]
                    link(n, nc.vector.tensor_tensor(rope_b[:, :, k, :], rot[:, :, k, :], bc(t, 1, MH + 1), ALU.mult))
                link(n, nc.vector.tensor_tensor(rot[:, :, 0, :], rope_a[:, :, 0, :], rope_b[:, :, 1, :], ALU.subtract))
                link(n, nc.vector.tensor_tensor(rot[:, :, 1, :], rope_b[:, :, 0, :], rope_a[:, :, 1, :], ALU.add))
                dve.sem_inc(s_qr, 1)
                nc.vector.tensor_copy(k_rows[:, :, NOPE:MD],
                                      q_rows[:, MH:MH + 1, NOPE:MD].to_broadcast([P, MH, ROPE])).then_inc(s_kr, 1)
                dve.wait_ge(s_mask, n + 1)
                dve.wait_ge(pb_free["a"], PB.done(n, "kTm"))
                past()
                rows(n, "kvup")

            def first(n, i):
                take(n, PA, pa_full, f"s{i}")
                if 2 <= i:
                    dve.wait_ge(s_p, n * HEADS + i - 1)
                    past()
                w = BLOCKS_SEEN(n) * P
                s, z = sc[:, i % 2, 0:w], pa[:, PA.slot(f"s{i}"), 0:w]
                if i < FH + MH:
                    nc.vector.tensor_tensor_reduce(s, z, mask[:, 0:w], -1.0, -NEG, ALU.add, ALU.min,
                                                   nmax[:, i:i + 1]).then_inc(pa_free["v"], 1)
                else:
                    link(n, nc.vector.tensor_tensor(s, z, mask[:, 1:w + 1], ALU.add))
                    dve.sem_inc(pa_free["v"], 1)
                    dve.wait_ge(pb_full, PB.full(n, f"p{i - 2}"))
                    nc.vector.scalar_tensor_tensor(out=pr[:, i % 2, 0:w], in0=s, scalar=-1.0, in1=s,
                                                   op0=ALU.mult, op1=ALU.min).then_inc(s_abs, 1)

            def second(n, i):
                k = i - FH - MH
                if k < 0:
                    return
                w = BLOCKS_SEEN(n) * P
                s, p = sc[:, i % 2, 0:w], pr[:, i % 2, 0:w]
                dve.wait_ge(s_sp, n * SH + k + 1)
                link(n, nc.vector.scalar_tensor_tensor(out=p, in0=s, scalar=0.0, in1=p, op0=ALU.max, op1=ALU.add))
                back = p[:, ::-1]
                link(n, nc.vector.tensor_tensor_scan(back, consts[:, K_LT + P - 1:K_LT + P].to_broadcast([P, w]),
                                                     back, 0.0, ALU.mult, ALU.add))
                nc.vector.tensor_tensor(p, s, p, ALU.subtract).then_inc(s_arg, 1)

            def attention(n):
                for i in range(HEADS + 1):
                    if i < HEADS:
                        first(n, i)
                    if i >= 1:
                        second(n, i - 1)
                    if i in HEAD_POINTS:
                        rows(n, f"head{i}")

            def output(n):
                layer = n // TILES
                dve.wait_ge(s_p, (n + 1) * HEADS)
                link(n, nc.vector.reciprocal(rinv[:, 0:FH + MH], rsum[:, 0:FH + MH]))
                rows(n, "y")
                dve.wait_ge(s_pv, (n + 1) * HEADS)
                past()
                link(n, nc.vector.tensor_tensor(
                    h[:, 0:FW + MW].rearrange("p (h d) -> p h d", d=HD),
                    yp[:, 0:FW + MW].rearrange("p (h d) -> p h d", d=HD),
                    bc(rinv[:, 0:FH + MH], 2, HD), ALU.mult))
                link(n, nc.vector.tensor_copy(h[:, FW + MW:D], yp[:, FW + MW:D]))
                dve.sem_inc(s_y, 1)
                dve.sem_inc(py_free["v"], 1)
                dve.wait_ge(s_ss, 4 * n + 3)
                link(n, variance(stat[:, 16:17], stat[:, 12:13], FW))
                link(n, variance(stat[:, 17:18], stat[:, 13:14], MW))
                variance(stat[:, 18:19], stat[:, 14:15], SW).then_inc(s_var, 1)
                refine(n, 3, stat[:, 16:19], stat[:, 20:23], stat[:, 23:26], stat[:, 26:29])
                for k, (a, b) in enumerate(((0, FW), (FW, FW + MW), (FW + MW, D))):
                    ins = nc.vector.tensor_scalar(h[:, a:b], h[:, a:b], stat[:, 23 + k:24 + k], None, ALU.mult)
                    if k == 2:
                        ins.then_inc(s_h, 1)
                    else:
                        link(n, ins)
                for j in range(2):
                    lab = f"yT{j}"
                    take(n, PB, pb_full, lab)
                    nc.vector.tensor_tensor(
                        hT[:, 4 * j:4 * j + 4, :], pb[:, PB.slot(lab), :].rearrange("p (a n) -> p a n", n=P),
                        bc(gT_out[:, bass.ds(layer, 1), 4 * j:4 * j + 4].rearrange("p a n -> p (a n)"), 2, P),
                        ALU.mult).then_inc(pb_free["v"], 1)
                rows(n, "z")
                for j in range(3):
                    i = 7 + j
                    c, w = BLOCKS[i][1], BLOCKS[i][2]
                    take(n, PA, pa_full, f"wo{j}")
                    xs = x_all[:, bass.ds(n % TILES, 1), c:c + w].rearrange("p a n -> p (a n)")
                    nc.vector.tensor_tensor(xs, xs, pa[:, PA.slot(f"wo{j}"), 0:w], ALU.add).then_inc(pa_free["v"], 1)
                rows(n, "wo")
                dve.wait_ge(s_ss, 4 * n + 4)
                variance(stat[:, 4:5], stat[:, 0:1], D).then_inc(s_var, 1)
                refine(n, 4, stat[:, 4:5], stat[:, 8:9], stat[:, 30:31], stat[:, 31:32])
                past()
                nc.vector.scalar_tensor_tensor(
                    out=h[:], in0=x_tile(n), scalar=stat[:, 30:31],
                    in1=ffn_gain[:, bass.ds(layer, 1), :].rearrange("p a n -> p (a n)"),
                    op0=ALU.mult, op1=ALU.mult).then_inc(s_h, 1)
                rows(n, "ffn")

            def best16(n, src, vals, idx):
                past()
                for a, b in ((0, 8), (8, 16)):
                    for s, v in zip(src, vals):
                        ins = nc.vector.max(v[:, a:b], s)
                    link(n, ins)
                    past()
                    for s, v, i in zip(src, vals, idx):
                        ins = nc.vector.max_index(i[:, a:b], v[:, a:b], s)
                    link(n, ins)
                    past()
                    if a == 0:
                        for s, v in zip(src, vals):
                            ins = nc.vector.match_replace(out=s, in_to_replace=v[:, a:b], in_values=s, imm_value=GONE)
                        link(n, ins)
                        past()

            def routing(n):
                layer = n // TILES
                for g in range(2):
                    rows(n, f"g{g}a")
                    if g == 0:
                        rows(n, "g0b")
                    dve.wait_ge(s_keys, 2 * n + g + 1)
                    best16(n, [key_s[:, k, :] for k in range(8)], [top[:, k, :] for k in range(8)],
                           [top_i[:, k, :] for k in range(8)])
                    link(n, nc.vector.tensor_copy(top_f[:], top_i[:]))
                    rows(n, "g0c" if g == 0 else "g1b")
                    pair = top[:].rearrange("p (h k) n -> p h k n", k=2)
                    for j in range(4):
                        ins = nc.vector.tensor_tensor(cand[:, j, :].rearrange("p (a b) -> p a b", b=TOPK),
                                                bc(pair[:, j, 0, :], 2, TOPK), bc(pair[:, j, 1, :], 1, TOPK), ALU.add)
                    link(n, ins)
                    bs = best[:, 4 * g:4 * g + 4, :]
                    best16(n, [cand[:, j, :] for j in range(4)], [bs[:, j, :] for j in range(4)],
                           [pos[:, j, :] for j in range(4)])
                    flat = pos[:].rearrange("p a n -> p (a n)")
                    nc.vector.tensor_scalar(pos_h[:, 0, :], flat, 4, None, ALU.logical_shift_right)
                    link(n, nc.vector.tensor_scalar(pos_h[:, 1, :], flat, TOPK - 1, None, ALU.bitwise_and))
                    link(n, nc.vector.tensor_copy(pos_f, pos_h))
                    rows(n, "g0d" if g == 0 else "g1c")
                    for k in range(2):
                        hot = cand[:].rearrange("p a n -> p (a n)").rearrange("p (m i) -> p m i", i=TOPK)
                        link(n, nc.vector.tensor_tensor(hot, bc(pos_f[:, k, :], 2, TOPK),
                                                        bc(iota16, 1, 4 * TOPK), ALU.is_equal))
                        for j in range(4):
                            hj = cand[:, j, :].rearrange("p (m i) -> p m i", i=TOPK)
                            ins = nc.vector.tensor_tensor(hj, hj, bc(top_f[:, 2 * j + k, :], 1, TOPK), ALU.mult)
                        link(n, ins)
                        link(n, nc.vector.tensor_reduce(key_f[:, k, :], hot, AX.X, ALU.add))
                    dve.sem_inc(s_keysfree, 1)
                    link(n, nc.vector.scalar_tensor_tensor(out=ids_f[:, HALF * g:HALF * (g + 1)], in0=key_f[:, 0, :],
                                                           scalar=float(NK), in1=key_f[:, 1, :],
                                                           op0=ALU.mult, op1=ALU.add))
                    past()
                    nc.vector.tensor_scalar(ids[:, bass.ds((n % 2) * PICKS + HALF * g, HALF)],
                                            ids_f[:, HALF * g:HALF * (g + 1)],
                                            layer_off[:, bass.ds(layer, 1)], None, ALU.add).then_inc(s_ids, 1)
                link(n, nc.vector.tensor_copy(gsum[:, 0, :], best[:, :, 0]))
                nc.vector.tensor_tensor(best[:], best[:], bc(gsum[:, 0, :], 2, TOPK), ALU.subtract).then_inc(s_best, 1)
                dve.wait_ge(s_bexp, n + 1)
                link(n, nc.vector.tensor_reduce(gsum[:, 0, :], best[:], AX.X, ALU.add))
                link(n, nc.vector.reciprocal(gsum[:, 1, :], gsum[:, 0, :]))

            def hand_over(n):
                link(n, nc.vector.tensor_tensor(
                    gates[:, bass.ds((n % 2) * PICKS, PICKS)].rearrange("p (h n) -> p h n", n=TOPK), best[:],
                    bc(gsum[:, 1, :], 2, TOPK), ALU.mult))
                dve.wait_ge(s_dot, n * PICKS + R)
                nc.vector.tensor_copy(h_dot[:], h[:])

            def dot_rows(m, it, q):
                for j in range(q * G, q * G + G):
                    if j % G == 0:
                        dve.wait_ge(s_gel, m * GROUPS + it * 2 + q + 1)
                    dve.wait_ge(s_u[j], (m * ITS + it + 1) * 16)
                    nc.vector.tensor_tensor_reduce(u_ring[:, j, :], u_ring[:, j, :], h_dot[:], 1.0, 0.0,
                                                   ALU.mult, ALU.add, dots[:, j:j + 1]).then_inc(s_dot, 1)

            def add_rows(m, it, q):
                k = m * GROUPS + it * 2 + q
                dve.wait_ge(s_coef, k + 1)
                for i in range(VE):
                    j = q * G + PE + i
                    dve.wait_ge(s_v[j], (m * ITS + it + 1) * 16)
                    dve.wait_ge(s_axpy, k * VE + i + 2 * VE)
                    past()
                    nc.vector.scalar_tensor_tensor(out=x_tile(m), in0=v_ring[:, j, :], scalar=coef[:, j:j + 1],
                                                   in1=x_tile(m), op0=ALU.mult, op1=ALU.add).then_inc(s_axpy, 1)

            def add_experts(m):
                dve.wait_ge(s_acc, m + 1)
                dve.wait_ge(s_axpy, (m + 1) * GROUPS * VE + 2 * VE)
                past()
                nc.vector.tensor_tensor(x_tile(m), x_tile(m), acc[:], ALU.add).then_inc(s_acc_free, 1)

            places = Places()

            def rows(n, label):
                if FIRST(n):
                    return
                p = places.next(label)
                dot_rows(n - 1, *divmod(p, 2))
                add_rows(n - 1, *divmod(p - 1, 2))

            dve.wait_ge(s_first, FIRST_LOADS)
            dve.wait_ge(s_zero, 9 + DEPTH)
            dve.sem_inc(s_dot, R)
            dve.sem_inc(s_gel, 2)
            dve.sem_inc(s_axpy, 2 * VE)
            dve.sem_inc(s_acc_free, 1)

            def step(n):
                mixer(n)
                attention(n)
                output(n)
                routing(n)
                rows(n, "g1d")
                hand_over(n)
                assert links[0] == DVE_LINKS, links
                if not FIRST(n):
                    add_rows(n - 1, *divmod(GROUPS - 1, 2))
                links[0] = 0
                norm(n + 1)
                dot_rows(n, 0, 0)
                if not FIRST(n):
                    add_experts(n - 1)

            norm(0)
            step(0)
            with dve.Fori(1, STEPS) as n:
                step(n)

            def final_norm(t):
                dve.wait_ge(s_ss, 4 * STEPS + 1 + t)
                variance(stat[:, 4:5], stat[:, 0:1], D).then_inc(s_var, 1)
                refine(STEPS, 1 + t, stat[:, 4:5], stat[:, 8:9], stat[:, 30:31], stat[:, 31:32])
                nc.vector.scalar_tensor_tensor(out=x_all[:, t, :], in0=x_all[:, t, :], scalar=stat[:, 30:31],
                                               in1=ffn_gain[:, 0, :], op0=ALU.mult, op1=ALU.mult).then_inc(s_fin, 1)

            dve.wait_ge(s_load, NLOADS + 16)
            dve.wait_ge(s_h, 4 * STEPS + 1)
            nc.vector.tensor_tensor(x_all[:, 0, :], h[:], ffn_gain[:, 0, :], ALU.mult).then_inc(s_fin, 1)
            for t in range(1, TILES - 1):
                final_norm(t)
            m = STEPS - 1
            dot_rows(m, 0, 1)
            add_rows(m, 0, 0)
            with dve.Fori(1, ITS) as it:
                dot_rows(m, it, 0)
                add_rows(m, it - 1, 1)
                dot_rows(m, it, 1)
                add_rows(m, it, 0)
            add_rows(m, ITS - 1, 1)
            add_experts(m)
            final_norm(TILES - 1)


def shape_constants():
    k = np.zeros((P, KW), np.float32)
    k[:, K_ID:K_ID + P] = np.eye(P, dtype=np.float32)
    s = np.arange(897)[None, :] - (TILES - 1) * P
    k[:, K_MASK:K_MASK + 897] = np.where(s <= np.arange(P)[:, None], 0.0, NEG)
    k[:, K_LT:K_LT + P] = np.triu(np.ones((P, P), np.float32))
    k[:, K_IOTA:K_IOTA + TOPK] = np.arange(TOPK)
    half = ROPE // 2
    inv = (1.0 / (np.float32(10000.0) ** (np.arange(half, dtype=np.float32) / np.float32(half)))).astype(np.float32)
    ang = np.arange(SEQ, dtype=np.float32)[:, None] * inv[None, :]
    cs = np.concatenate([np.cos(ang), np.sin(ang)], axis=1).astype(np.float32)
    k[:, K_ROPE:] = cs.reshape(TILES, P, ROPE).transpose(1, 0, 2).reshape(P, TILES * ROPE)
    return k


def kernel(**inputs):
    import concourse.bacc as _bacc
    from concourse.bass_utils import run_bass_kernel_spmd as _run

    def parts(a):
        a = np.asarray(a)
        return np.ascontiguousarray(a.reshape(a.shape[0], -1, P).transpose(2, 0, 1))

    i = {k: np.asarray(v) for k, v in inputs.items()}
    data = {
        "x": i["x"], "w_in": i["w_in"],
        "w_in_kf": np.concatenate([i["w_in"][:, :, C_KR:C_KR + ROPE], i["w_in"][:, :, C_FL:C_FL + FH]], axis=2)
        .reshape(DEPTH, KC, P, ROPE + FH).transpose(0, 2, 1, 3).reshape(DEPTH, P, KC * (ROPE + FH)),
        "fgate_b": i["fgate_b"], "attn_gT": parts(i["attn_norm_g"]),
        "lat_gT": parts(np.concatenate([i["mla_q_norm_g"], i["mla_kv_norm_g"]], axis=1)),
        "out_gT": parts(np.concatenate([i["out_norm_fox"], i["out_norm_mla"], i["out_norm_sb"]], axis=1)),
        "ffn_g": i["ffn_norm_g"], "final_g": i["final_norm_g"], "w_uq": i["w_uq"], "w_ukv": i["w_ukv"],
        "w_out": i["w_out"], "w_q": i["peer_w_query"],
        "keys_T": np.stack([i["peer_keys1"], i["peer_keys2"]], axis=1).transpose(3, 0, 1, 2),
        "u": i["peer_u"].reshape(DEPTH * EXPERTS, D), "v": i["peer_v"].reshape(DEPTH * EXPERTS, D),
        "consts": shape_constants(),
    }
    nc = _bacc.Bacc("TRN2", target_bir_lowering=False, num_devices=1)
    arrays, args = {}, []
    for name, a in data.items():
        a = np.ascontiguousarray(a)
        arrays[f"in_{name}_dram"] = a
        args.append(nc.dram_tensor(f"in_{name}_dram", a.shape, mybir.dt.from_np(a.dtype), kind="ExternalInput").ap())
    out = nc.dram_tensor("out_0_dram", (1, SEQ, D), F32, kind="ExternalOutput").ap()
    trunk(nc, *args, out)
    r = _run(nc, [arrays], core_ids=[0])
    return r.results[0]["out_0_dram"]
```
